# Optimizing a Trainium2 kernel written in Bass

```python
import math
import jax, jax.numpy as jnp
from jax import lax
import numpy as np

D_MODEL = 1024
BATCH = 1
SEQ = 1024
DEPTH = 2

GRID_W = 64
CTX_LEN = 256
MIX_WIDTH = 2 * D_MODEL
DH_A = 128
H_A = (MIX_WIDTH // 2) // DH_A
W_A = H_A * DH_A
W_B = MIX_WIDTH - W_A
DN_CHUNK = 64
DN_CONV_W = 3
SC_CONV_W = 3
DH_C = 64
H_C = MIX_WIDTH // (2 * DH_C)
W_C = H_C * 2 * DH_C
Q_BLOCK = 128
ROPE_THETA = 10000.0
RMS_EPS = 1e-6
L2_EPS = 1e-6
N_EVEN = (DEPTH + 1) // 2
N_ODD = DEPTH // 2
EVEN_COLS = 4 * W_A + 4 * H_A + 4 * W_B
ODD_COLS = 4 * W_C

kernel_name = 'hybrid_deltanet_shortconv_diffattn_prefix_trunk'

def rmsnorm(x, w):
    xf = x.astype(jnp.float32)
    y = xf * lax.rsqrt(jnp.mean(xf * xf, axis=-1, keepdims=True) + RMS_EPS)
    return (y * w.astype(jnp.float32)).astype(x.dtype)

def l2norm(x):
    return x * lax.rsqrt(jnp.sum(x * x, axis=-1, keepdims=True) + L2_EPS)

def split_cols(p, sizes):
    parts, start = [], 0
    for s in sizes:
        parts.append(p[..., start:start + s])
        start += s
    return parts

def centred_conv(x, w):
    pad = w.shape[0] // 2
    return lax.conv_general_dilated(
        x, w.astype(x.dtype)[:, None, :], window_strides=(1,), padding=[(pad, pad)],
        dimension_numbers=('NWC', 'WIO', 'NWC'), feature_group_count=x.shape[-1])

def adaln(cvec, w_mod, b_mod):
    m = jax.nn.silu(cvec) @ w_mod + b_mod
    return jnp.split(m, 3, axis=-1)

def axial_rope_tables(n_tok, dtype):
    rows = n_tok // GRID_W
    row = jnp.repeat(jnp.arange(rows), GRID_W).astype(jnp.float32)
    col = jnp.tile(jnp.arange(GRID_W), rows).astype(jnp.float32)
    half = DH_C // 2
    inv = ROPE_THETA ** (-jnp.arange(0, half, 2, dtype=jnp.float32) / half)
    ang_r = row[:, None] * inv
    ang_c = col[:, None] * inv
    ang = jnp.concatenate([ang_r, ang_r, ang_c, ang_c], axis=-1)
    return jnp.cos(ang).astype(dtype), jnp.sin(ang).astype(dtype)

def rope2d(x, cos, sin):
    h = x.shape[-1] // 2
    q = h // 2
    xr, xc = x[..., :h], x[..., h:]
    rot = jnp.concatenate([-xr[..., q:], xr[..., :q], -xc[..., q:], xc[..., :q]], axis=-1)
    return x * cos[:, None, None, :] + rot * sin[:, None, None, :]

def gated_delta_chunked(q, k, v, g, beta, s0):
    b, h, t, dk = q.shape
    dv = v.shape[-1]
    cs = DN_CHUNK
    n = t // cs
    chunks = lambda u: u.reshape(b, h, n, cs, *u.shape[3:])
    q, k, v, g, beta = chunks(q), chunks(k), chunks(v), chunks(g), chunks(beta)
    gcum = jnp.cumsum(g, axis=-1)
    causal = jnp.tril(jnp.ones((cs, cs), bool))
    strict = jnp.tril(jnp.ones((cs, cs), bool), -1)
    diff = gcum[..., :, None] - gcum[..., None, :]
    decay = jnp.where(causal, jnp.exp(jnp.where(causal, diff, 0.0)), 0.0)
    kb = k * beta[..., None]
    a_mat = jnp.where(strict, jnp.einsum('bhnid,bhnjd->bhnij', kb, k) * decay, 0.0)
    tmat = a_mat + jnp.eye(cs, dtype=a_mat.dtype)
    rhs = jnp.concatenate([v * beta[..., None], kb * jnp.exp(gcum)[..., None]], axis=-1)
    sol = lax.linalg.triangular_solve(tmat, rhs, left_side=True, lower=True, unit_diagonal=True)
    u, w = sol[..., :dv], sol[..., dv:]
    qk = jnp.where(causal, jnp.einsum('bhnid,bhnjd->bhnij', q, k) * decay, 0.0)
    qg = q * jnp.exp(gcum)[..., None]
    kd = k * jnp.exp(gcum[..., -1:] - gcum)[..., None]
    glast = jnp.exp(gcum[..., -1])

    def step(s, xs):
        u_n, w_n, qg_n, qk_n, kd_n, gl_n = xs
        v_new = u_n - jnp.einsum('bhcd,bhde->bhce', w_n, s)
        o_n = jnp.einsum('bhcd,bhde->bhce', qg_n, s) + jnp.einsum('bhcj,bhje->bhce', qk_n, v_new)
        s = s * gl_n[..., None, None] + jnp.einsum('bhcd,bhce->bhde', kd_n, v_new)
        return s, o_n

    xs = tuple(jnp.moveaxis(u_, 2, 0) for u_ in (u, w, qg, qk, kd, glast))
    s, o = lax.scan(step, s0, xs)
    o = jnp.moveaxis(o, 0, 2).reshape(b, h, t, dv)
    return o, s

def dn_prep(qkv_raw, a_raw, b_raw, conv_w, a_log, dt_bias):
    bsz, t = qkv_raw.shape[:2]
    qkv = jax.nn.silu(centred_conv(qkv_raw, conv_w))
    q, k, v = jnp.split(qkv, 3, axis=-1)
    heads = lambda u: jnp.swapaxes(u.reshape(bsz, t, H_A, DH_A), 1, 2).astype(jnp.float32)
    q = l2norm(heads(q)) * (DH_A ** -0.5)
    k = l2norm(heads(k))
    v = heads(v)
    a = a_raw.astype(jnp.float32).reshape(bsz, t, 2, H_A)
    bb = b_raw.astype(jnp.float32).reshape(bsz, t, 2, H_A)
    g = -jnp.exp(a_log.astype(jnp.float32)) * jax.nn.softplus(a + dt_bias.astype(jnp.float32))
    beta = jax.nn.sigmoid(bb)
    to_dir = lambda u: jnp.transpose(u, (2, 0, 3, 1))
    return q, k, v, to_dir(g), to_dir(beta)

def even_mixer(hx, hc, w_in, conv_w, a_log, dt_bias, norm_w, sc_w, w_out, with_ctx_out):
    n_ctx = hc.shape[1]
    proj = jnp.concatenate([hc, hx], axis=1) @ w_in
    sizes = (3 * W_A, W_A, 2 * H_A, 2 * H_A, W_B, W_B, W_B, W_B)
    pc = split_cols(proj[:, :n_ctx], sizes)
    px = split_cols(proj[:, n_ctx:], sizes)
    qc, kc, vc, gc, bc = dn_prep(pc[0], pc[2], pc[3], conv_w, a_log, dt_bias)
    qx, kx, vx, gx, bx = dn_prep(px[0], px[2], px[3], conv_w, a_log, dt_bias)
    s0 = jnp.zeros((hx.shape[0], H_A, DH_A, DH_A), jnp.float32)
    flip = lambda u: jnp.flip(u, axis=2)
    o_cf, s_f = gated_delta_chunked(qc, kc, vc, gc[0], bc[0], s0)
    o_cb, s_b = gated_delta_chunked(flip(qc), flip(kc), flip(vc), flip(gc[1]), flip(bc[1]), s0)
    o_xf, _ = gated_delta_chunked(qx, kx, vx, gx[0], bx[0], s_f)
    o_xb, _ = gated_delta_chunked(flip(qx), flip(kx), flip(vx), flip(gx[1]), flip(bx[1]), s_b)

    def branch_a(o, z):
        bsz, _, t, _ = o.shape
        o = rmsnorm(jnp.swapaxes(o, 1, 2), norm_w)
        zz = z.reshape(bsz, t, H_A, DH_A).astype(jnp.float32)
        return (o * jax.nn.silu(zz)).reshape(bsz, t, W_A).astype(z.dtype)

    def branch_b(p):
        bg, cg, xin, zb = p[4], p[5], p[6], p[7]
        return bg * centred_conv(cg * xin, sc_w) * jax.nn.silu(zb)

    y_x = jnp.concatenate([branch_a(o_xf + flip(o_xb), px[1]), branch_b(px)], axis=-1)
    out_x = y_x @ w_out
    if not with_ctx_out:
        return out_x, None
    y_c = jnp.concatenate([branch_a(o_cf + flip(o_cb), pc[1]), branch_b(pc)], axis=-1)
    return out_x, y_c @ w_out

def diff_attend(q, k, v, lam):
    s = jnp.einsum('bqhmd,bkhmd->bhmqk', q, k, preferred_element_type=jnp.float32)
    p = jax.nn.softmax(s, axis=-1)
    a = p[:, :, 0] - lam * p[:, :, 1]
    return jnp.einsum('bhqk,bkhe->bqhe', a.astype(v.dtype), v)

def odd_mixer(hx, hc, w_in, lam_vecs, subln_w, w_out, lam_init, with_ctx_out):
    n_ctx = hc.shape[1]
    proj = jnp.concatenate([hc, hx], axis=1) @ w_in

    def heads(p):
        bsz, t = p.shape[:2]
        q, k, v, z = jnp.split(p, 4, axis=-1)
        return (q.reshape(bsz, t, H_C, 2, DH_C) * (DH_C ** -0.5), k.reshape(bsz, t, H_C, 2, DH_C),
                v.reshape(bsz, t, H_C, 2 * DH_C), z.reshape(bsz, t, H_C, 2 * DH_C))

    qc, kc, vc, zc = heads(proj[:, :n_ctx])
    qx, kx, vx, zx = heads(proj[:, n_ctx:])
    bsz, t_lat = hx.shape[:2]
    cos, sin = axial_rope_tables(t_lat, hx.dtype)
    qx = rope2d(qx, cos, sin)
    kx = rope2d(kx, cos, sin)
    lv = lam_vecs.astype(jnp.float32)
    lam = jnp.exp(jnp.sum(lv[0] * lv[1])) - jnp.exp(jnp.sum(lv[2] * lv[3])) + lam_init
    k_all = jnp.concatenate([kc, kx], axis=1)
    v_all = jnp.concatenate([vc, vx], axis=1)
    n_blk = t_lat // Q_BLOCK
    q_blocks = jnp.moveaxis(qx.reshape(bsz, n_blk, Q_BLOCK, H_C, 2, DH_C), 1, 0)
    o_x = lax.map(lambda qb: diff_attend(qb, k_all, v_all, lam), q_blocks)
    o_x = jnp.moveaxis(o_x, 0, 1).reshape(bsz, t_lat, H_C, 2 * DH_C)

    def post(o, z):
        y = rmsnorm(o, subln_w) * (1.0 - lam_init) * jax.nn.silu(z)
        return y.reshape(z.shape[0], z.shape[1], W_C)

    out_x = post(o_x, zx) @ w_out
    if not with_ctx_out:
        return out_x, None
    o_c = diff_attend(qc, kc, vc, lam)
    return out_x, post(o_c, zc) @ w_out

def setup_inputs(seed: int = 0) -> dict:
    key = jax.random.key(seed)
    ks = jax.random.split(key, 20)
    f32 = jnp.float32

    def nrm(k, shape, scale):
        return jax.random.normal(k, shape, f32) * scale

    a_log = jnp.log(jax.random.uniform(ks[8], (N_EVEN, 2, H_A), f32, 1.0, 16.0))
    dt = jnp.exp(jax.random.uniform(ks[9], (N_EVEN, 2, H_A), f32, math.log(1e-3), math.log(1e-1)))
    dt_bias = dt + jnp.log(-jnp.expm1(-dt))
    return {
        'x': nrm(ks[0], (BATCH, SEQ, D_MODEL), 1.0),
        'c': nrm(ks[1], (BATCH, D_MODEL), 1.0),
        'ctx': nrm(ks[2], (BATCH, CTX_LEN, D_MODEL), 1.0),
        'c_ctx': nrm(ks[3], (D_MODEL,), 1.0),
        'norm_w': 1.0 + nrm(ks[4], (DEPTH, D_MODEL), 0.02),
        'mod_w': nrm(ks[5], (DEPTH, D_MODEL, 3 * D_MODEL), 0.5 * D_MODEL ** -0.5),
        'mod_b': nrm(ks[6], (DEPTH, 3 * D_MODEL), 0.01),
        'even_w_in': nrm(ks[7], (N_EVEN, D_MODEL, EVEN_COLS), D_MODEL ** -0.5),
        'even_dn_conv_w': nrm(ks[10], (N_EVEN, DN_CONV_W, 3 * W_A), DN_CONV_W ** -0.5),
        'even_dn_a_log': a_log,
        'even_dn_dt_bias': dt_bias,
        'even_dn_norm_w': 1.0 + nrm(ks[11], (N_EVEN, DH_A), 0.02),
        'even_sc_conv_w': nrm(ks[12], (N_EVEN, SC_CONV_W, W_B), SC_CONV_W ** -0.5),
        'even_w_out': nrm(ks[13], (N_EVEN, W_A + W_B, D_MODEL), (W_A + W_B) ** -0.5),
        'odd_w_in': nrm(ks[14], (N_ODD, D_MODEL, ODD_COLS), D_MODEL ** -0.5),
        'odd_lambda': nrm(ks[15], (N_ODD, 4, DH_C), 0.1),
        'odd_subln_w': 1.0 + nrm(ks[16], (N_ODD, 2 * DH_C), 0.02),
        'odd_w_out': nrm(ks[17], (N_ODD, W_C, D_MODEL), W_C ** -0.5),
        'final_norm_w': 1.0 + nrm(ks[18], (D_MODEL,), 0.02),
    }

def reference(x, c, ctx, c_ctx, norm_w, mod_w, mod_b, even_w_in, even_dn_conv_w, even_dn_a_log,
              even_dn_dt_bias, even_dn_norm_w, even_sc_conv_w, even_w_out, odd_w_in, odd_lambda,
              odd_subln_w, odd_w_out, final_norm_w):
    for layer in range(DEPTH):
        last = layer == DEPTH - 1
        sh_x, sc_x, g_x = (m[:, None, :] for m in adaln(c, mod_w[layer], mod_b[layer]))
        sh_c, sc_c, g_c = adaln(c_ctx, mod_w[layer], mod_b[layer])
        hx = rmsnorm(x, norm_w[layer]) * (1.0 + sc_x) + sh_x
        hc = rmsnorm(ctx, norm_w[layer]) * (1.0 + sc_c) + sh_c
        i = layer // 2
        if layer % 2 == 0:
            out_x, out_c = even_mixer(hx, hc, even_w_in[i], even_dn_conv_w[i], even_dn_a_log[i],
                                      even_dn_dt_bias[i], even_dn_norm_w[i], even_sc_conv_w[i],
                                      even_w_out[i], not last)
        else:
            lam_init = 0.8 - 0.6 * math.exp(-0.3 * layer)
            out_x, out_c = odd_mixer(hx, hc, odd_w_in[i], odd_lambda[i], odd_subln_w[i], odd_w_out[i],
                                     lam_init, not last)
        x = x + g_x * out_x
        if not last:
            ctx = ctx + g_c * out_c
    return rmsnorm(x, final_norm_w)


_drawn_inputs = setup_inputs


def setup_inputs(seed=0):
    import zlib

    import numpy as np

    out = dict(_drawn_inputs(seed))
    spreads = {}
    factors = {'ctx': 11.684,
     'norm_w': 6.774,
     'mod_b': 4.991,
     'even_dn_norm_w': 200.0,
     'odd_lambda': 4.22,
     'odd_subln_w': 200.0,
     'final_norm_w': 22.675,
     'c_ctx': 4.157,
     'even_dn_conv_w': 3.064,
     'even_dn_a_log': 8.0,
     'even_dn_dt_bias': 8.0}
    for name, (base, spread) in spreads.items():
        noise = np.random.default_rng([zlib.crc32(name.encode()), seed]).standard_normal(out[name].shape)
        drawn = base * np.exp(spread * noise) if base else spread * noise
        out[name] = __import__('jax').numpy.asarray(drawn.astype(out[name].dtype))
    for name, factor in factors.items():
        out[name] = (out[name] * factor).astype(out[name].dtype)
    return out
```

```python
import math
from contextlib import ExitStack, contextmanager

import concourse.bass as bass
from concourse import mybir

F32 = mybir.dt.float32
F32R = mybir.dt.float32r
U32 = mybir.dt.uint32
ALU = mybir.AluOpType
ACT = mybir.ActivationFunctionType
AX = mybir.AxisListType

P = 128
D = 1024
KC = D // P
T_CTX, T_LAT = 256, 1024
T = T_CTX + T_LAT
TILES = T // P
CTX_TILES = T_CTX // P
LAT_TILES = T_LAT // P
EPS = 1e-6


class Count:

    def __init__(self, sem):
        self.sem, self.base, self.local, self.index, self.per = sem, 0, 0, None, 0

    def value(self):
        if self.index is None:
            return self.base + self.local
        return self.index * self.per + (self.base + self.local)

    def loop(self, index, per):
        self.base, self.local, self.index, self.per = self.base + self.local, 0, index, per

    def end(self, n):
        assert self.local == self.per, (self.local, self.per)
        self.base, self.local, self.index = self.base + n * self.per, 0, None


def link(eng, count, ins):
    ins.then_inc(count.sem, 1)
    count.local += 1
    eng.wait_ge(count.sem, count.value())


@contextmanager
def semaphores(nc):
    handles = []

    def new(name):
        handles.append(nc.alloc_semaphore(name=name))
        return handles[-1]
    yield new
    nc.all_engine_barrier()
    nc.clear_and_free_semaphores(handles)
    nc.all_engine_barrier()


def modulation(nc, sems, layer, A, mods):
    G = 512
    NG = 3 * D // G
    with ExitStack() as ph:
        sb = lambda n, s, d=F32: ph.enter_context(nc.sbuf_tensor(f"{n}_{layer}", s, d))
        ident2 = sb("ident2", [2, 2])
        cond = sb("cond", [P, 2, KC])
        scond = sb("scond", [P, KC, 2])
        bias, rows = sb("mod_bias", [2, 3 * D]), sb("mod_rows", [2, 3 * D])
        w = [sb(f"mod_w{i}", [P, KC, G]) for i in range(2)]
        acc = [ph.enter_context(nc.psum_tensor(f"mod_acc{i}_{layer}", [2, G], F32)) for i in range(2)]
        turned = ph.enter_context(nc.psum_tensor(f"mod_turned_{layer}", [P, 2 * KC, 2], F32))
        sem = lambda n: sems(f"{n}_{layer}")
        cond_in, cond_ready, out_dma = sem("cond_in"), sem("cond_ready"), sem("mods_out")
        w_in = [sem(f"mod_w_in{i}") for i in range(2)]
        acc_ready, row_ready, all_turned, mods_ready = map(sem, ("mod_acc_ready", "mod_row_ready", "mod_all_turned", "mods_ready"))
        block = ph.enter_context(nc.Block())
        wv = A["mod_w"][layer, :, :].rearrange("(k p) (g n) -> p g k n", p=P, n=G)

        @block.sync
        def _(sp):
            sp.dma_start(cond[:, 0, :], A["c"]).then_inc(cond_in, 16)
            sp.dma_start(cond[:, 1, :], A["c_ctx"]).then_inc(cond_in, 16)
            sp.dma_start(ident2[:, :], A["identity"][0:2, 0:2]).then_inc(cond_in, 16)
            sp.dma_start(bias[:, :], A["mod_b"][layer, :].partition_broadcast(2)).then_inc(cond_in, 16)
            for b in range(2):
                sp.dma_start(w[b][:, :, :], wv[:, b, :, :]).then_inc(w_in[b], 16)
            with sp.Fori(1, NG // 2) as i:
                for b in range(2):
                    sp.wait_ge(acc_ready, i * 2 + (b - 1))
                    sp.dma_start(w[b][:, :, :], wv[:, bass.ds(i * 2 + b, 1), :, :].rearrange(
                        "p a k n -> p (a k) n")).then_inc(w_in[b], 16)
            sp.wait_ge(row_ready, NG)
            sp.dma_start(A["mods_dram"][layer, :, :], rows[:, 2 * D:3 * D]).then_inc(out_dma, 16)
            sp.wait_ge(out_dma, 16)

        @block.scalar
        def _(act):
            act.wait_ge(cond_in, 64)
            nc.scalar.activation(scond[:, :, :].rearrange("p k s -> p s k"), cond[:, :, :], ACT.Silu)\
                .then_inc(cond_ready, 1)

        @block.tensor
        def _(pe):
            def group(i, b, first):
                pe.wait_ge(w_in[b], i * 16 + 16)
                if not first:
                    pe.wait_ge(row_ready, i * 2 + (b - 1))
                for k in range(KC):
                    mm = nc.tensor.matmul(acc[b][:, :], scond[:, k, :], w[b][:, k, :], start=(k == 0), stop=(k == KC - 1))
                mm.then_inc(acc_ready, 1)

            pe.wait_ge(cond_ready, 1)
            for b in range(2):
                group(0, b, True)
            with pe.Fori(1, NG // 2) as i:
                for b in range(2):
                    group(i, b, False)
            pe.wait_ge(row_ready, NG)
            for j in range(2 * KC):
                mm = nc.tensor.transpose(turned[:, j, :], rows[:, j * P:(j + 1) * P], ident2[:, :])
            mm.then_inc(all_turned, 1)

        @block.vector
        def _(dve):
            dve.wait_ge(cond_in, 64)
            with dve.Fori(0, NG // 2) as i:
                for b in range(2):
                    dve.wait_ge(acc_ready, i * 2 + (b + 1))
                    g = bass.ds(i * (2 * G) + b * G, G)
                    nc.vector.tensor_tensor(rows[:, g], acc[b][:, :], bias[:, g], ALU.add).then_inc(row_ready, 1)
            dve.wait_ge(all_turned, 1)
            nc.vector.tensor_copy(mods[:, layer, :, :], turned[:, :, :]).then_inc(mods_ready, 1)
            dve.wait_ge(mods_ready, 1)


def normalise(nc, sems, layer, A, mods, h_hi, h_lo, rows):
    with ExitStack() as ph:
        sb = lambda n, s, d=F32: ph.enter_context(nc.sbuf_tensor(f"{n}_n{layer}", s, d))
        ident = sb("ident", [P, P])
        norm_w = sb("norm_w", [P, KC])
        coef = sb("coef", [P, KC, 2])
        mhalf = sb("mhalf", [P, 1])
        xt = [sb(f"xt{b}", [P, D]) for b in range(2)]
        xn = [sb(f"xn{b}", [P, D]) for b in range(2)]
        ssq = [sb(f"ssq{b}", [P, 1]) for b in range(2)]
        ms = [sb(f"ms{b}", [P, 1]) for b in range(2)]
        rstd = [sb(f"rstd{b}", [P, 1]) for b in range(2)]
        hf = [sb(f"hf{b}", [P, KC, P]) for b in range(2)]
        xT = [ph.enter_context(nc.psum_tensor(f"xT{b}_n{layer}", [P, KC, P], F32)) for b in range(2)]
        sem = lambda n: sems(f"{n}_n{layer}")
        const_in, coef_ready, half_ready = sem("const_in"), sem("coef_ready"), sem("half_ready")
        x_in = [sem(f"x_in{b}") for b in range(2)]
        ssq_ready, ms_ready, rstd_ready, xn_ready = sem("ssq_ready"), sem("ms_ready"), sem("rstd_ready"), sem("xn_ready")
        xT_ready, hf_ready, hi_ready, lo_ready = sem("xT_ready"), sem("hf_ready"), sem("hi_ready"), sem("lo_ready")
        block = ph.enter_context(nc.Block())

        def pairs(eng, *parts):
            for part in parts:
                for b in range(2):
                    part(b, b, True, 1)
            with eng.Fori(1, TILES // 2) as i:
                for part in parts:
                    for b in range(2):
                        part(i * 2 + b, b, False, 0)

        @block.sync
        def _(sp):
            sp.dma_start(ident[:, :], A["identity"]).then_inc(const_in, 16)
            sp.dma_start(norm_w[:, :], A["norm_w"][:, layer, :]).then_inc(const_in, 16)

            def load(n, b, first, stream):
                if not first:
                    sp.wait_ge(xn_ready, n - 1)
                sp.dma_start(xt[b][:, :], rows.rearrange("(t p) d -> t p d", p=P)[bass.ds(n, 1), :, :].rearrange(
                    "a p d -> (a p) d")).then_inc(x_in[b], 16)
            pairs(sp, load)

        @block.scalar
        def _(act):
            def scale(n, b, first, stream):
                act.wait_ge(x_in[b], (n - b) * 8 + 16)
                if not first:
                    act.wait_ge(xT_ready, n - 1)
                    act.wait_ge(rstd_ready, n - 1)
                nc.scalar.activation(xn[b][:, :], xt[b][:, :], ACT.Square, accum_out=ssq[b][:, :]).then_inc(ssq_ready, 1)
                act.wait_ge(rstd_ready, n + 1)
                act.wait_ge(ssq_ready, n + 1)
                nc.scalar.activation(xn[b][:, :], xt[b][:, :], ACT.Copy, scale=rstd[b][:, :]).then_inc(xn_ready, 1)

            def high(n, b, first, stream):
                act.wait_ge(hf_ready, n + 1)
                nc.scalar.activation(h_hi[:, :, bass.ds(n * P, P)], hf[b][:, :, :], ACT.Copy).then_inc(hi_ready, 1)

            pairs(act, scale, high)

        @block.gpsimd
        def _(pool):
            nc.gpsimd.memset(mhalf[:, :], -0.5).then_inc(half_ready, 1)
            pool.wait_ge(half_ready, 1)

            def root(n, b, first, stream):
                pool.wait_ge(ms_ready, n + 1)
                nc.gpsimd.tensor_tensor(rstd[b][:, :], ms[b][:, :], mhalf[:, :], ALU.pow).then_inc(rstd_ready, 1)
            pairs(pool, root)

        @block.tensor
        def _(pe):
            pe.wait_ge(const_in, 32)

            def turn(n, b, first, stream):
                pe.wait_ge(xn_ready, n + 1)
                if not first:
                    pe.wait_ge(hf_ready, n - 1)
                for k in range(KC):
                    mm = nc.tensor.transpose(xT[b][:, k, :], xn[b][:, k * P:(k + 1) * P], ident[:, :])
                mm.then_inc(xT_ready, 1)
            pairs(pe, turn)

        @block.vector
        def _(dve):
            dve.wait_ge(const_in, 32)
            for s in range(2):
                ins = nc.vector.scalar_tensor_tensor(coef[:, :, s], mods[:, layer, KC:2 * KC, s], 1.0, norm_w[:, :],
                                                     ALU.add, ALU.mult)
            ins.then_inc(coef_ready, 1)
            dve.wait_ge(coef_ready, 1)

            def mean(n, b, first, stream):
                dve.wait_ge(ssq_ready, n + 1)
                nc.vector.tensor_scalar(ms[b][:, :], ssq[b][:, :], 1.0 / D, EPS, ALU.mult, ALU.add).then_inc(ms_ready, 1)

            def shift(n, b, first, stream):
                dve.wait_ge(xT_ready, n + 1)
                if not first:
                    dve.wait_ge(lo_ready, n - 1)
                for k in range(KC):
                    ins = nc.vector.tensor_scalar(hf[b][:, k, :], xT[b][:, k, :], coef[:, k, stream:stream + 1],
                                                  mods[:, layer, k, stream:stream + 1], ALU.mult, ALU.add)
                ins.then_inc(hf_ready, 1)
                dve.wait_ge(hi_ready, n + 1)
                nc.vector.tensor_tensor(h_lo[:, :, bass.ds(n * P, P)], hf[b][:, :, :],
                                        h_hi[:, :, bass.ds(n * P, P)].bitcast(F32), ALU.subtract).then_inc(lo_ready, 1)
            pairs(dve, mean, shift)


def project_even(nc, sems, A, h_hi, h_lo):
    NQ, NZ, NG = 24, 8, 8
    NB = NQ + NZ + 4 * NG + 1
    with ExitStack() as ph:
        sb = lambda n, s, d=F32: ph.enter_context(nc.sbuf_tensor(f"{n}_e", s, d))
        conv_w = sb("conv_w", [P, 3, NQ])
        sc_w = sb("sc_w", [P, 3, NG])
        w = [sb(f"w{b}", [P, KC, P]) for b in range(2)]
        w_hi = [sb(f"w_hi{b}", [P, KC, P], F32R) for b in range(2)]
        w_lo = [sb(f"w_lo{b}", [P, KC, P], F32R) for b in range(2)]
        raw = [sb(f"raw{b}", [P, T]) for b in range(2)]
        conv = [sb(f"conv{b}", [P, T]) for b in range(2)]
        bc = [sb(f"branch{g}", [P, T]) for g in range(4)]
        acc = [ph.enter_context(nc.psum_tensor(f"acc{b}_e", [P, 1536], F32)) for b in range(2)]
        sem = lambda n: sems(f"{n}_e")
        const_in = sem("const_in")
        w_in = [sem(f"w_in{b}") for b in range(2)]
        w_hi_ready, w_lo_ready, product, acc_read = sem("w_hi_ready"), sem("w_lo_ready"), sem("product"), sem("acc_read")
        conv_done, vstep, group_done = sem("conv_done"), sem("vstep"), sem("group_done")
        out_dma = [sem(f"out_dma{b}") for b in range(2)]
        y_dma = sem("y_dma")
        block = ph.enter_context(nc.Block())
        w_dram = A["even_w_in"]
        conv_dram = A["conv_dram"].rearrange("(n p) t -> n p t", p=P)
        z_dram = A["z_dram"].rearrange("(n p) t -> n p t", p=P)
        y_dram = A["y_dram"].rearrange("(n p) t -> n p t", p=P)
        one = lambda ap, n: ap[bass.ds(n, 1), :, :].rearrange("a p t -> (a p) t")

        @block.sync
        def _(sp):
            sp.dma_start(conv_w[:, :, :], A["even_dn_conv_w"]).then_inc(const_in, 16)
            sp.dma_start(sc_w[:, :, :], A["even_sc_conv_w"]).then_inc(const_in, 16)

            def load(n, b, first):
                if not first:
                    sp.wait_ge(w_lo_ready, n - 1)
                sp.dma_start(w[b][:, :, :], w_dram[bass.ds(n, 1), :, :, :].rearrange("a p k n -> (a p) k n"))\
                    .then_inc(w_in[b], 16)
            def pair(i, first=False):
                for b in range(2):
                    load(i * 2 + b, b, first)
            pair(0, True)
            pair(1)
            with sp.Fori(2, NQ // 2 + 2) as i:
                pair(i)
                for b in range(2):
                    sp.wait_ge(conv_done, i * 2 + (b - 3))
                    sp.dma_start(one(conv_dram, i * 2 + (b - 4)), conv[b][:, :]).then_inc(out_dma[b], 16)
            with sp.Fori(NQ // 2 + 2, (NQ + NZ) // 2 + 2) as i:
                pair(i)
                for b in range(2):
                    sp.wait_ge(acc_read, i * 2 + (b - 3))
                    sp.dma_start(one(z_dram, i * 2 + (b - 4 - NQ)), raw[b][:, :]).then_inc(out_dma[b], 16)

            def store_y(j):
                sp.wait_ge(group_done, j + 1)
                sp.dma_start(one(y_dram, j + 8), conv[1][:, :]).then_inc(y_dma, 16)
            with sp.Fori(0, NG - 1) as j:
                pair(j * 2 + ((NQ + NZ) // 2 + 2))
                pair(j * 2 + ((NQ + NZ) // 2 + 3))
                store_y(j)
            load(NB - 1, 0, False)
            store_y(NG - 1)
            sp.wait_ge(acc_read, NB)
            sp.dma_start(A["ab_dram"], raw[0][0:32, :]).then_inc(out_dma[0], 16)
            sp.wait_ge(out_dma[0], 8 * (NQ + NZ) + 16)
            sp.wait_ge(out_dma[1], 8 * (NQ + NZ))
            sp.wait_ge(y_dma, 16 * NG)

        @block.tensor
        def _(pe):
            def multiply(n, b, first):
                pe.wait_ge(w_lo_ready, n + 1)
                if not first:
                    pe.wait_ge(acc_read, n - 1)
                products(nc, acc[b], w_hi[b], w_lo[b], h_hi, h_lo, 0, T).then_inc(product, 1)
            multiply(0, 0, True)
            multiply(1, 1, True)
            with pe.Fori(1, NB // 2) as i:
                multiply(i * 2, 0, False)
                multiply(i * 2 + 1, 1, False)
            multiply(NB - 1, 0, False)

        @block.scalar
        def _(act):
            def high(n, b, first):
                act.wait_ge(w_in[b], (n - b) * 8 + 16)
                if not first:
                    act.wait_ge(product, n - 1)
                nc.scalar.activation(w_hi[b][:, :, :], w[b][:, :, :], ACT.Copy).then_inc(w_hi_ready, 1)

            def evacuate(n, b, dst, fn):
                act.wait_ge(product, n + 1)
                nc.scalar.activation(dst[:, :], acc[b][:, 0:T], fn).then_inc(acc_read, 1)

            high(0, 0, True)
            high(1, 1, True)
            evacuate(0, 0, raw[0], ACT.Copy)
            high(2, 0, False)
            evacuate(1, 1, raw[1], ACT.Copy)
            with act.Fori(1, NQ // 2) as i:
                for b in range(2):
                    high(i * 2 + (b + 1), 1 - b, False)
                    act.wait_ge(conv_done, i * 2 + (b - 1))
                    evacuate(i * 2 + b, b, raw[b], ACT.Copy)
            with act.Fori(0, NZ // 2) as i:
                for b in range(2):
                    n = i * 2 + (NQ + b)
                    high(n + 1, 1 - b, False)
                    act.wait_ge(conv_done, NQ - 1 + b)
                    act.wait_ge(out_dma[b], i * 16 + 16 * (NQ // 2))
                    evacuate(n, b, raw[b], ACT.Silu)

            def group(j, first):
                for g in range(4):
                    n = j * 4 + (NQ + NZ + g)
                    high(n + 1, (g + 1) % 2, False)
                    if not first:
                        act.wait_ge(group_done, j)
                    evacuate(n, g % 2, bc[g], ACT.Silu if g == 3 else ACT.Copy)
            group(0, True)
            with act.Fori(1, NG) as j:
                group(j, False)
            act.wait_ge(out_dma[0], 8 * (NQ + NZ))
            evacuate(NB - 1, 0, raw[0], ACT.Copy)

        @block.vector
        def _(dve):
            dve.wait_ge(const_in, 32)
            step = Count(vstep)

            def low(n, b, first):
                dve.wait_ge(w_hi_ready, n + 1)
                nc.vector.tensor_tensor(w_lo[b][:, :, :], w[b][:, :, :], w_hi[b][:, :, :].bitcast(F32),
                                        ALU.subtract).then_inc(w_lo_ready, 1)

            def convolve(dst, src, wt):
                link(dve, step, nc.vector.tensor_scalar(dst[:, :], src[:, :], wt[1], None, ALU.mult))
                for a, b in ((0, T_CTX), (T_CTX, T)):
                    ins = nc.vector.scalar_tensor_tensor(dst[:, a + 1:b], src[:, a:b - 1], wt[0], dst[:, a + 1:b],
                                                         ALU.mult, ALU.add)
                link(dve, step, ins)
                for a, b in ((0, T_CTX), (T_CTX, T)):
                    ins = nc.vector.scalar_tensor_tensor(dst[:, a:b - 1], src[:, a + 1:b], wt[2], dst[:, a:b - 1],
                                                         ALU.mult, ALU.add)
                return ins

            def taps(wt, j):
                return [wt[:, t, bass.ds(j, 1)] for t in range(3)]

            def qkv(n, b, first):
                dve.wait_ge(acc_read, n + 1)
                if not first:
                    dve.wait_ge(out_dma[b], (n - b) * 8)
                convolve(conv[b], raw[b], taps(conv_w, n)).then_inc(conv_done, 1)

            low(0, 0, True)
            for b in range(2):
                low(b + 1, 1 - b, False)
                qkv(b, b, True)
            with dve.Fori(1, NQ // 2) as i:
                step.loop(i - 1, 4)
                for b in range(2):
                    low(i * 2 + (b + 1), 1 - b, False)
                    qkv(i * 2 + b, b, False)
            step.end(NQ // 2 - 1)
            with dve.Fori(0, NZ // 2) as i:
                for b in range(2):
                    low(i * 2 + (NQ + b + 1), 1 - b, False)

            def group(j, first):
                for g in range(4):
                    low(j * 4 + (NQ + NZ + g + 1), (g + 1) % 2, False)
                dve.wait_ge(acc_read, j * 4 + (NQ + NZ + 4))
                dve.wait_ge(out_dma[0], 8 * (NQ + NZ))
                dve.wait_ge(out_dma[1], 8 * (NQ + NZ))
                link(dve, step, nc.vector.tensor_tensor(bc[1][:, :], bc[1][:, :], bc[2][:, :], ALU.mult))
                link(dve, step, convolve(conv[0], bc[1], taps(sc_w, j)))
                link(dve, step, nc.vector.tensor_tensor(conv[0][:, :], conv[0][:, :], bc[0][:, :], ALU.mult))
                if not first:
                    dve.wait_ge(y_dma, j * 16)
                nc.vector.tensor_tensor(conv[1][:, :], conv[0][:, :], bc[3][:, :], ALU.mult).then_inc(group_done, 1)
            step.base, step.local = step.base + step.local, 0
            group(0, True)
            with dve.Fori(1, NG) as j:
                step.base, step.local = step.base + step.local, 0
                step.loop(j - 1, 5)
                group(j, False)
            step.end(NG - 1)


def products(nc, acc, w_hi, w_lo, h_hi, h_lo, t0, t1, chunks=KC):
    for k in range(chunks):
        for lhs, rhs in ((w_hi, h_hi), (w_hi, h_lo), (w_lo, h_hi)):
            for a in range(t0, t1, 512):
                b = min(a + 512, t1)
                mm = nc.tensor.matmul(acc[:, a - t0:b - t0], lhs[:, k, :], rhs[:, k, a:b],
                                      start=(k == 0 and rhs is h_hi and lhs is w_hi),
                                      stop=(k == chunks - 1 and lhs is w_lo))
    return mm


VECS = 8
GC, R2, EG, NEG_EG, NBETA, BETA, BETA_KD, GL = range(VECS)
H_A = 8
CH = 64
HT = H_A * TILES
BLK = 16


def decay_vectors(nc, sems, A, vt):
    HORNER = [1.0 / (2 * k + 1) for k in range(9, 0, -1)]
    with ExitStack() as ph:
        sb = lambda n, s, d=F32: ph.enter_context(nc.sbuf_tensor(f"{n}_d", s, d))
        ident = sb("ident", [P, P])
        consts = sb("consts", [HT, 4])
        names = ("a", "b", "x", "ax", "e", "s", "s2", "poly", "g", "inner", "gc", "r2", "ega", "kda", "eb", "beta", "nbeta",
                 "eg", "neg_eg", "kd", "beta_kd")
        v = {n: sb(n, [HT, 2, P]) for n in names}
        gla, gl, neg_a = sb("gla", [HT, 2]), sb("gl", [HT, 2]), sb("neg_a", [HT, 2])
        turned = [ph.enter_context(nc.psum_tensor(f"turned{i}_d", [P, 4, P], F32)) for i in range(4)]
        sem = lambda n: sems(f"{n}_d")
        ab_in, astep, vstep, turn_done = sem("ab_in"), sem("astep"), sem("vstep"), sem("turn_done")
        args_ready, vectors_ready = sem("args_ready"), sem("vectors_ready")
        block = ph.enter_context(nc.Block())
        ABS_E, EXP_B, EXP_A, EXP_EG, EXP_KD, EXP_GL = 2, 3, 4, 5, 6, 7

        @block.sync
        def _(sp):
            ab = A["ab_dram"].rearrange("(v d h) (n t) -> v h n d t", v=2, d=2, t=P)
            for h in range(H_A):
                for j, dst in enumerate((v["a"], v["b"])):
                    sp.dma_start(dst[h * TILES:(h + 1) * TILES, :, :], ab[j, h]).then_inc(ab_in, 16)
            sp.dma_start(ident[:, :], A["identity"]).then_inc(ab_in, 16)
            sp.dma_start(consts[:, :], A["decay_consts"]).then_inc(ab_in, 16)

        @block.scalar
        def _(act):
            step = Count(astep)
            act.wait_ge(ab_in, 16 * (2 * H_A + 2))
            for d in range(2):
                ins = nc.scalar.activation(v["ax"][:, d, :], v["a"][:, d, :], ACT.Abs, bias=consts[:, d:d + 1])
            link(act, step, ins)
            link(act, step, nc.scalar.activation(v["e"][:, :, :], v["ax"][:, :, :], ACT.Exp, scale=-1.0))
            link(act, step, nc.scalar.activation(v["eb"][:, :, :], v["b"][:, :, :], ACT.Exp, scale=-1.0))
            link(act, step, nc.scalar.activation(neg_a[:, :], consts[:, 2:4], ACT.Exp))
            act.wait_ge(args_ready, 1)
            link(act, step, nc.scalar.activation(v["eg"][:, :, :], v["ega"][:, :, :], ACT.Exp))
            link(act, step, nc.scalar.activation(v["kd"][:, :, :], v["kda"][:, :, :], ACT.Exp))
            link(act, step, nc.scalar.activation(gl[:, :], gla[:, :], ACT.Exp))
            act.wait_ge(turn_done, 16)
            for b in range(4):
                ins = nc.scalar.activation(vt[:, 2 * b:2 * b + 2, :, :].rearrange("p v d n -> p (v d) n"),
                                           turned[b][:, :, 0:HT], ACT.Copy)
            ins.then_inc(astep, 1)

        @block.vector
        def _(dve):
            step = Count(vstep)
            tt = lambda out, a, b, op: link(dve, step, nc.vector.tensor_tensor(out, a, b, op))
            ts = lambda out, a, s1, s2, o1, o2: link(dve, step, nc.vector.tensor_scalar(out, a, s1, s2, o1, o2))
            stt = lambda out, a, s, b, o1, o2: link(dve, step, nc.vector.scalar_tensor_tensor(out, a, s, b, o1, o2))
            full = lambda n: v[n][:, :, :]
            dve.wait_ge(ab_in, 16 * (2 * H_A + 2))
            for d in range(2):
                ts(v["x"][:, d, :], v["a"][:, d, :], consts[:, d:d + 1], 0.0, ALU.add, ALU.max)
            dve.wait_ge(astep, ABS_E)
            ts(full("s"), full("e"), 2.0, None, ALU.add, ALU.bypass)
            link(dve, step, nc.vector.reciprocal(full("s2"), full("s")))
            tt(full("s"), full("e"), full("s2"), ALU.mult)
            tt(full("s2"), full("s"), full("s"), ALU.mult)
            ts(full("poly"), full("s2"), HORNER[0], None, ALU.mult, ALU.bypass)
            for c in HORNER[1:]:
                stt(full("poly"), full("poly"), c, full("s2"), ALU.add, ALU.mult)
            stt(full("poly"), full("poly"), 1.0, full("s"), ALU.add, ALU.mult)
            stt(full("x"), full("poly"), 2.0, full("x"), ALU.mult, ALU.add)
            dve.wait_ge(astep, EXP_A)
            for d in range(2):
                ts(v["g"][:, d, :], v["x"][:, d, :], neg_a[:, d:d + 1], -1.0, ALU.mult, ALU.mult)
            ts(full("eb"), full("eb"), 1.0, None, ALU.add, ALU.bypass)
            link(dve, step, nc.vector.reciprocal(full("beta"), full("eb")))
            ts(full("nbeta"), full("beta"), -1.0, None, ALU.mult, ALU.bypass)
            blocks = lambda u, d: u[:, d, :].rearrange("p (c k n) -> p c k n", k=CH // BLK, n=BLK)
            for i in range(BLK):
                for d in range(2):
                    at, before = (i, i - 1) if d == 0 else (BLK - 1 - i, BLK - i)
                    x, y = blocks(v["g"], d), blocks(v["inner"], d)
                    if i == 0:
                        ins = nc.vector.tensor_copy(y[:, :, :, at], x[:, :, :, at])
                    else:
                        ins = nc.vector.tensor_tensor(y[:, :, :, at], y[:, :, :, before], x[:, :, :, at], ALU.add)
                link(dve, step, ins)
            for i in range(CH // BLK):
                for d in range(2):
                    k, prev, last = (i, i - 1, BLK - 1) if d == 0 else (CH // BLK - 1 - i, CH // BLK - i, 0)
                    y, out = blocks(v["inner"], d), blocks(v["gc"], d)
                    if i == 0:
                        ins = nc.vector.tensor_copy(out[:, :, k, :], y[:, :, k, :])
                    else:
                        for c in range(2):
                            ins = nc.vector.tensor_scalar(out[:, c, k, :], y[:, c, k, :], out[:, c, prev, last:last + 1],
                                                          None, ALU.add)
                link(dve, step, ins)
            for d, cf, cs, tf, te in ((0, 0, 1, CH - 1, P - 1), (1, 1, 0, CH, 0)):
                F, S = slice(cf * CH, (cf + 1) * CH), slice(cs * CH, (cs + 1) * CH)
                gc = v["gc"][:, d, :]
                tot_f, tot_s = v["gc"][:, d, tf:tf + 1], v["gc"][:, d, te:te + 1]
                ts(v["r2"][:, d, F], gc[:, F], tot_f, None, ALU.subtract, ALU.bypass)
                link(dve, step, nc.vector.tensor_copy(v["r2"][:, d, S], gc[:, S]))
                link(dve, step, nc.vector.tensor_copy(v["ega"][:, d, F], gc[:, F]))
                ts(v["ega"][:, d, S], gc[:, S], tot_f, None, ALU.add, ALU.bypass)
                ts(v["kda"][:, d, S], gc[:, S], -1.0, tot_s, ALU.mult, ALU.add)
                ts(v["kda"][:, d, F], gc[:, F], -1.0, tot_f, ALU.mult, ALU.add)
                ts(v["kda"][:, d, F], v["kda"][:, d, F], tot_s, None, ALU.add, ALU.bypass)
                ins = nc.vector.tensor_tensor(gla[:, d:d + 1], tot_f, tot_s, ALU.add)
            ins.then_inc(args_ready, 1)
            dve.wait_ge(astep, EXP_GL)
            ts(full("neg_eg"), full("eg"), -1.0, None, ALU.mult, ALU.bypass)
            nc.vector.tensor_tensor(full("beta_kd"), full("beta"), full("kd"), ALU.mult).then_inc(vectors_ready, 1)

        @block.tensor
        def _(pe):
            pe.wait_ge(ab_in, 16 * (2 * H_A + 2))
            pe.wait_ge(astep, EXP_GL)
            pe.wait_ge(vectors_ready, 1)
            order = ["gc", "r2", "eg", "neg_eg", "nbeta", "beta", "beta_kd", None]
            for j, name in enumerate(order):
                for d in range(2):
                    src = v[name][:, d, :] if name else gl[:, d:d + 1].to_broadcast([HT, P])
                    nc.tensor.transpose(turned[j // 2][:, (j % 2) * 2 + d, 0:HT], src, ident[0:HT, 0:HT])\
                        .then_inc(turn_done, 1)


LEVELS = [1 << s for s in range(7)]
BT = 2
SWEEP = [list(range(TILES)), list(range(CTX_TILES - 1, -1, -1)) + list(range(TILES - 1, CTX_TILES - 1, -1))]


def deltanet(nc, sems, A, vt):
    NBAT = TILES // BT
    NL = len(LEVELS) - 1
    LANES = [(0, 1), (2, 3), (4,)]
    SLOTS = 2 + 2 * NL
    ROUNDS = len(LANES)
    END = 3 * TILES
    with ExitStack() as ph:
        sb = lambda n, s, d=F32: ph.enter_context(nc.sbuf_tensor(f"{n}_r", s, d))
        ident, eye4 = sb("ident", [P, P]), sb("eye4", [P, 4, P])
        causal = sb("causal", [P, 2, P])
        lower = sb("lower", [P, len(LEVELS), 2, P], U32)
        upper = sb("upper", [P, len(LEVELS), 2, P], U32)
        norm_w, mhalf = sb("norm_w", [P, 1]), sb("mhalf", [P, 2 * TILES])
        cv, gate = sb("cv", [P, 3, T]), sb("gate", [P, T])
        sq = sb("sq", [P, TILES, 2, P])
        ssq, rn = sb("ssq", [P, TILES, 2]), sb("rn", [P, TILES, 2])
        vh = [sb(f"vh{b}", [P, VECS, 2, TILES]) for b in range(2)]
        tok = [sb(f"tok{b}", [P, TILES, 3, P]) for b in range(2)]
        kq = [sb(f"kq{b}", [P, TILES, 2, P]) for b in range(2)]
        yy = [sb(f"yy{b}", [P, TILES, 2, P]) for b in range(2)]
        qk = [sb(f"qk{b}", [P, TILES, 2, P]) for b in range(2)]
        dm = [sb(f"dm{l}", [P, BT, 2, P]) for l in range(2)]
        dec = [sb(f"dec{l}", [P, BT, 2, P]) for l in range(2)]
        at = [sb(f"at{l}", [P, BT, 2, P]) for l in range(2)]
        xx = [sb(f"xx{l}", [P, BT, 2, P]) for l in range(2)]
        pp = [sb(f"pp{l}", [P, BT, 2, P]) for l in range(2)]
        state = sb("state", [P, 2, P])
        rr, vn, vk, oq = (sb(n, [P, 2, P]) for n in ("rr", "vn", "vk", "oq"))
        od = sb("od", [P, 2, TILES, P])
        yt = sb("yt", [P, T])
        ossq, orn = sb("ossq", [P, TILES]), sb("orn", [P, TILES])
        bank = [ph.enter_context(nc.psum_tensor(f"bank{i}_r", [P, 4, P], F32)) for i in range(8)]
        flips = [bank[3 * l] for l in range(2)]
        halves = [bank[3 * l + 1] for l in range(2)]
        yprod = [bank[3 * l + 2] for l in range(2)]
        prep = bank[3:6]
        near, far = bank[6], bank[7]
        sem = lambda n: sems(f"{n}_r")
        const_in, cv_in, gate_in, y_out = sem("const_in"), sem("cv_in"), sem("gate_in"), sem("y_out")
        silu_done, turned, tok_ready, sq_ready, ssq_ready, rn_ready = map(
            sem, ("silu_done", "turned", "tok_ready", "sq_ready", "ssq_ready", "rn_ready"))
        normed, back, kq_ready = map(sem, ("normed", "back", "kq_ready"))
        gram, dm_ready, dec_ready, at_ready, at_turned, eye_ready = map(
            sem, ("gram", "dm_ready", "dec_ready", "at_ready", "at_turned", "eye_ready"))
        xy_ready, p_done, p_ready, xy_done = map(sem, ("xy_ready", "p_done", "p_ready", "xy_done"))
        ks_done, r_ready, oq_ready, xr_done, vk_ready, o_done, state_ready = map(
            sem, ("ks_done", "r_ready", "oq_ready", "xr_done", "vk_ready", "o_done", "state_ready"))
        o_sum, osq_ready, ossq_ready, orn_ready, oscaled, o_turned, o_gated, vh_ready = map(
            sem, ("o_sum", "osq_ready", "ossq_ready", "orn_ready", "oscaled", "o_turned", "o_gated", "vh_ready"))
        half_ready, sq_summed, osq_summed, passed = map(sem, ("half_ready", "sq_summed", "osq_summed", "passed"))
        block = ph.enter_context(nc.Block())
        flat = lambda t: t[:, :, :, :].rearrange("p a d n -> p (a d) n")
        sys4 = lambda t, n: t[:, BT * n:BT * n + BT, :, :].rearrange("p a d n -> p (a d) n")
        TURNS = {END + g: range(3 * g, min(3 * g + 3, TILES)) for g in range(-(-TILES // 3))}
        BACKS = {END + 7: range(0, 6), END + 9: range(6, TILES)}
        OUTS = {END + 8: range(0, 8), END + 10: range(8, TILES)}
        assert END + 10 < ROUNDS * SLOTS and END >= (ROUNDS - 1) * SLOTS

        def heads(eng, inverses, beside):
            for j in range(ROUNDS * SLOTS):
                beside(-1, 1, j, False, True)
            inverses(0, 0, False, True)
            with eng.Fori(0, H_A // 2 - 1) as i:
                inverses(i * 2 + 1, 1, True, True)
                inverses(i * 2 + 2, 0, True, True)
            inverses(H_A - 1, 1, True, False)
            for j in range(ROUNDS * SLOTS):
                beside(H_A, 0, j, True, False)

        @block.sync
        def _(sp):
            for dst, src in ((ident[:, :], "identity"), (eye4[:, :, :], "eye4"), (causal[:, :, :], "causal"),
                             (lower[:, :, :, :], "lower"), (upper[:, :, :, :], "upper"), (norm_w[:, :], "even_dn_norm_w")):
                sp.dma_start(dst, A[src]).then_inc(const_in, 16)
            qkv = A["conv_dram"].rearrange("(s h p) t -> h p s t", s=3, p=P)
            zd = A["z_dram"].rearrange("(h p) t -> h p t", p=P)
            yd = A["y_dram"].rearrange("(h p) t -> h p t", p=P)

            def load(h):
                sp.dma_start(cv[:, :, :], qkv[bass.ds(h, 1), :, :, :].rearrange("a p s t -> (a p) s t")).then_inc(cv_in, 16)

            def load_gate(h):
                sp.dma_start(gate[:, :], zd[bass.ds(h, 1), :, :].rearrange("a p t -> (a p) t")).then_inc(gate_in, 16)

            def store(h):
                sp.wait_ge(o_gated, h * 2 + 2)
                sp.dma_start(yd[bass.ds(h, 1), :, :].rearrange("a p t -> (a p) t"), yt[:, :]).then_inc(y_out, 16)
            load(0)
            load_gate(0)
            for h in range(2):
                sp.wait_ge(turned, h * TILES + TILES)
                load(h + 1)
            store(0)
            with sp.Fori(2, H_A - 1) as h:
                sp.wait_ge(turned, h * TILES + TILES)
                load(h + 1)
                sp.wait_ge(y_out, h * 16 - 16)
                load_gate(h - 1)
                store(h - 1)
            for h in (H_A - 1, H_A):
                sp.wait_ge(y_out, h * 16 - 16)
                load_gate(h - 1)
                store(h - 1)
            sp.wait_ge(y_out, 16 * H_A)

        @block.gpsimd
        def _(pool):
            nc.gpsimd.memset(mhalf[:, :], -0.5).then_inc(half_ready, 1)
            pool.wait_ge(half_ready, 1)

            def norms(h):
                pool.wait_ge(ssq_ready, h + 1)
                nc.gpsimd.tensor_tensor(rn[:, :, :].rearrange("p t s -> p (t s)"), ssq[:, :, :].rearrange("p t s -> p (t s)"),
                                        mhalf[:, :], ALU.pow).then_inc(rn_ready, 1)

            def outputs(h):
                pool.wait_ge(state_ready, h * (TILES + 1) + (TILES + 1))
                nc.gpsimd.tensor_tensor(od[:, 0, :, :], od[:, 0, :, :], od[:, 1, :, :], ALU.add).then_inc(o_sum, 1)
                pool.wait_ge(ossq_ready, h + 1)
                nc.gpsimd.tensor_tensor(orn[:, :], ossq[:, :], mhalf[:, 0:TILES], ALU.pow).then_inc(orn_ready, 1)
            norms(0)
            norms(1)
            with pool.Fori(1, H_A - 1) as h:
                outputs(h - 1)
                norms(h + 1)
            outputs(H_A - 2)
            outputs(H_A - 1)

        @block.scalar
        def _(act):
            def beside(h, b, j, scan, prepare):
                s, g = h - 1, h + 1
                if scan and j < END and j % 3 == 0:
                    k = j // 3
                    act.wait_ge(ks_done, s * TILES + (k + 1))
                    act.wait_ge(state_ready, s * (TILES + 1) + (k + 1))
                    for d in range(2):
                        ins = nc.scalar.activation(oq[:, d, :], far[:, d, :], ACT.Copy,
                                                   scale=vh[1 - b][:, EG, d, SWEEP[d][k]:SWEEP[d][k] + 1])
                    ins.then_inc(oq_ready, 1)
                if prepare and END - 8 <= j < END - 5:
                    c = j - (END - 8)
                    if c == 0:
                        act.wait_ge(cv_in, g * 16 + 16)
                    nc.scalar.activation(cv[:, c, :], cv[:, c, :], ACT.Silu).then_inc(silu_done, 1)
                if scan and j == END + 1:
                    act.wait_ge(o_sum, s + 1)
                    nc.scalar.activation(od[:, 1, :, :], od[:, 0, :, :], ACT.Square).then_inc(osq_ready, 1)
                if prepare and j in TURNS:
                    for t in TURNS[j]:
                        act.wait_ge(turned, g * TILES + (t + 1))
                        nc.scalar.activation(tok[1 - b][:, t, :, :], prep[t % 3][:, 0:3, :], ACT.Copy).then_inc(tok_ready, 1)
                if prepare and j == END + 4:
                    act.wait_ge(tok_ready, g * TILES + TILES)
                    act.wait_ge(ssq_ready, g)
                    nc.scalar.activation(sq[:, :, :, :], tok[1 - b][:, :, 0:2, :], ACT.Square).then_inc(sq_ready, 1)
                if prepare and j in BACKS:
                    for t in BACKS[j][::2]:
                        act.wait_ge(back, g * (TILES // 2) + (t // 2 + 1))
                        nc.scalar.activation(kq[1 - b][:, t:t + 2, :, :].rearrange("p a s n -> p (a s) n"),
                                             prep[t // 2 % 3][:, :, :], ACT.Copy).then_inc(kq_ready, 1)

            def inverses(h, b, scan, prepare):
                for r, lanes in enumerate(LANES):
                    for l, n in enumerate(lanes):
                        act.wait_ge(dm_ready, h * NBAT + (n + 1))
                        nc.scalar.activation(flat(dec[l]), flat(dm[l]), ACT.Exp).then_inc(dec_ready, 1)
                    beside(h, b, r * SLOTS, scan, prepare)
                    beside(h, b, r * SLOTS + 1, scan, prepare)
                    for s in range(NL):
                        for l, n in enumerate(lanes):
                            act.wait_ge(p_done, h * (NBAT * NL) + (1 + level_at(lanes, s, l, NL)))
                            nc.scalar.activation(flat(pp[l]), halves[l][:, :, :], ACT.Copy).then_inc(p_ready, 1)
                        beside(h, b, r * SLOTS + 2 * s + 2, scan, prepare)
                        beside(h, b, r * SLOTS + 2 * s + 3, scan, prepare)
            heads(act, inverses, beside)

        @block.tensor
        def _(pe):
            pe.wait_ge(const_in, 96)

            def beside(h, b, j, scan, prepare):
                s, g, o = h - 1, h + 1, 1 - b
                k = j // 3
                if scan and j < END and j % 3 == 0:
                    pe.wait_ge(state_ready, s * (TILES + 1) + (k + 1))
                    for i in range(2):
                        for d in range(2):
                            mm = nc.tensor.matmul((near, far)[i][:, d, :], kq[o][:, SWEEP[d][k], i, :], state[:, d, :],
                                                  start=True, stop=True)
                    mm.then_inc(ks_done, 1)
                if scan and j < END and j % 3 == 1:
                    pe.wait_ge(r_ready, s * TILES + (k + 1))
                    for d in range(2):
                        mm = nc.tensor.matmul(near[:, 2 + d, :], yy[o][:, SWEEP[d][k], d, :], rr[:, d, :], start=True, stop=True)
                    mm.then_inc(xr_done, 1)
                if scan and j < END and j % 3 == 2:
                    pe.wait_ge(vk_ready, s * TILES + (k + 1))
                    pe.wait_ge(oq_ready, s * TILES + (k + 1))
                    for d in range(2):
                        nc.tensor.matmul(near[:, d, :], tok[o][:, SWEEP[d][k], 1, :], vk[:, d, :], start=True, stop=True)
                    for d in range(2):
                        mm = nc.tensor.matmul(far[:, 2 + d, :], qk[o][:, SWEEP[d][k], d, :], vn[:, d, :], start=True, stop=True)
                    mm.then_inc(o_done, 1)
                if scan and j in OUTS:
                    pe.wait_ge(oscaled, s + 1)
                    if OUTS[j][0]:
                        pe.wait_ge(o_gated, s * 2 + 1)
                    for t in OUTS[j]:
                        mm = nc.tensor.transpose(bank[6 + t // 4 % 2][:, t % 4, :], od[:, 1, t, :], ident[:, :])
                    mm.then_inc(o_turned, 1)
                if prepare and j in TURNS:
                    if j == END:
                        pe.wait_ge(silu_done, g * 3 + 3)
                    for t in TURNS[j]:
                        if t >= 3:
                            pe.wait_ge(tok_ready, g * TILES + (t - 2))
                        for c in range(3):
                            mm = nc.tensor.transpose(prep[t % 3][:, c, :], cv[:, c, t * P:(t + 1) * P], ident[:, :])
                        mm.then_inc(turned, 1)
                if prepare and j in BACKS:
                    pe.wait_ge(normed, g + 1)
                    for t in BACKS[j]:
                        if t >= 6 and t % 2 == 0:
                            pe.wait_ge(kq_ready, g * (TILES // 2) + (t // 2 - 2))
                        for i in range(2):
                            mm = nc.tensor.transpose(prep[t // 2 % 3][:, t % 2 * 2 + i, :], tok[o][:, t, 1 - i, :], ident[:, :])
                        if t % 2:
                            mm.then_inc(back, 1)

            def inverses(h, b, scan, prepare):
                pe.wait_ge(kq_ready, h * (TILES // 2) + TILES // 2)
                pe.wait_ge(vh_ready, h + 1)
                for r, lanes in enumerate(LANES):
                    for l, n in enumerate(lanes):
                        if r:
                            pe.wait_ge(xy_ready, xy_value(h, n - 2, NL, NL))
                        elif l == 0 and scan:
                            pe.wait_ge(xy_ready, xy_value(h - 1, NBAT - 1, NL, NL))
                        for a in range(BT):
                            t = BT * n + a
                            nc.tensor.matmul(halves[l][:, 2 * a:2 * a + 2, :], kq[b][:, t, 0, :], kq[b][:, t, :, :],
                                             start=True, stop=True)
                        for a in range(BT):
                            for d in range(2):
                                t = BT * n + a
                                mm = nc.tensor.transpose(flips[l][:, 2 * a + d, :],
                                                         vh[b][:, GC, d, t:t + 1].to_broadcast([P, P]), ident[:, :])
                        mm.then_inc(gram, 1)
                    beside(h, b, r * SLOTS, scan, prepare)
                    for l, n in enumerate(lanes):
                        pe.wait_ge(at_ready, h * NBAT + (n + 1))
                        for j in range(4):
                            mm = nc.tensor.transpose(flips[l][:, j, :], flat(at[l])[:, j, :], ident[:, :])
                        mm.then_inc(at_turned, 1)
                    beside(h, b, r * SLOTS + 1, scan, prepare)
                    for s in range(1, NL + 1):
                        for l, n in enumerate(lanes):
                            pe.wait_ge(xy_ready, xy_value(h, n, s - 1, NL))
                            for j in range(4):
                                mm = nc.tensor.matmul(halves[l][:, j, :], flat(at[l])[:, j, :], flat(xx[l])[:, j, :],
                                                      start=True, stop=True)
                            mm.then_inc(p_done, 1)
                        beside(h, b, r * SLOTS + 2 * s, scan, prepare)
                        for l, n in enumerate(lanes):
                            pe.wait_ge(p_ready, h * (NBAT * NL) + (1 + level_at(lanes, s - 1, l, NL)))
                            y4 = sys4(yy[b], n)
                            if s < NL:
                                for j in range(4):
                                    nc.tensor.matmul(flips[l][:, j, :], y4[:, j, :], flat(pp[l])[:, j, :],
                                                     start=True, stop=True)
                            for j in range(4):
                                mm = nc.tensor.matmul(yprod[l][:, j, :], flat(pp[l])[:, j, :], y4[:, j, :],
                                                      start=True, stop=True)
                            mm.then_inc(xy_done, 1)
                        beside(h, b, r * SLOTS + 2 * s + 1, scan, prepare)
            heads(pe, inverses, beside)

        @block.vector
        def _(dve):
            dve.wait_ge(const_in, 96)

            def beside(h, b, j, scan, prepare):
                s, g, o = h - 1, h + 1, 1 - b
                k = j // 3
                if scan and j == 0:
                    nc.vector.memset(state[:, :, :], 0.0).then_inc(state_ready, 1)
                if scan and j < END and j % 3 == 0:
                    dve.wait_ge(ks_done, s * TILES + (k + 1))
                    for d in range(2):
                        t = SWEEP[d][k]
                        ins = nc.vector.scalar_tensor_tensor(rr[:, d, :], near[:, d, :], vh[o][:, NEG_EG, d, t:t + 1],
                                                             tok[o][:, t, 2, :], ALU.mult, ALU.add)
                    ins.then_inc(r_ready, 1)
                if scan and j < END and j % 3 == 1:
                    dve.wait_ge(xr_done, s * TILES + (k + 1))
                    for d in range(2):
                        t = SWEEP[d][k]
                        nc.vector.tensor_scalar(vn[:, d, :], near[:, 2 + d, :], vh[o][:, BETA, d, t:t + 1], None, ALU.mult)
                        ins = nc.vector.tensor_scalar(vk[:, d, :], near[:, 2 + d, :], vh[o][:, BETA_KD, d, t:t + 1], None, ALU.mult)
                    ins.then_inc(vk_ready, 1)
                if scan and j < END and j % 3 == 2:
                    dve.wait_ge(o_done, s * TILES + (k + 1))
                    dve.wait_ge(state_ready, s * (TILES + 1) + (k + 1))
                    for d in range(2):
                        t = SWEEP[d][k]
                        ins = nc.vector.scalar_tensor_tensor(state[:, d, :], state[:, d, :], vh[o][:, GL, d, t:t + 1],
                                                             near[:, d, :], ALU.mult, ALU.add)
                    dve.wait_ge(oq_ready, s * TILES + (k + 1))
                    for d in range(2):
                        ins = nc.vector.tensor_tensor(od[:, d, SWEEP[d][k], :], far[:, 2 + d, :], oq[:, d, :], ALU.add)
                    ins.then_inc(state_ready, 1)
                if scan and j == END + 2:
                    dve.wait_ge(osq_ready, s + 1)
                    nc.vector.tensor_reduce(ossq[:, :], od[:, 1, :, :], AX.X, ALU.add).then_inc(osq_summed, 1)
                    dve.wait_ge(osq_summed, s + 1)
                    nc.vector.tensor_scalar(ossq[:, :], ossq[:, :], 1.0 / P, EPS, ALU.mult, ALU.add).then_inc(ossq_ready, 1)
                if scan and j == END + 4:
                    dve.wait_ge(orn_ready, s + 1)
                    for t in range(TILES):
                        ins = nc.vector.tensor_scalar(od[:, 1, t, :], od[:, 0, t, :], orn[:, t:t + 1], None, ALU.mult)
                    ins.then_inc(oscaled, 1)
                if scan and j in OUTS:
                    first = OUTS[j][0] == 0
                    dve.wait_ge(o_turned, s * 2 + (1 if first else 2))
                    if first:
                        dve.wait_ge(gate_in, s * 16 + 16)
                    for t0 in range(OUTS[j][0], OUTS[j][-1] + 1, 4):
                        t1 = min(t0 + 4, TILES)
                        ins = nc.vector.scalar_tensor_tensor(
                            yt[:, t0 * P:t1 * P], bank[6 + t0 // 4 % 2][:, 0:t1 - t0, :].rearrange("p a n -> p (a n)"),
                            norm_w[:, 0:1], gate[:, t0 * P:t1 * P], ALU.mult, ALU.mult)
                    ins.then_inc(o_gated, 1)
                if prepare and j == END + 5:
                    nc.vector.tensor_copy(vh[o][:, :, :, :], vt[:, :, :, bass.ds(g * TILES, TILES)]).then_inc(vh_ready, 1)
                    dve.wait_ge(sq_ready, g + 1)
                    dve.wait_ge(rn_ready, g)
                    nc.vector.tensor_reduce(ssq[:, :, :], sq[:, :, :, :], AX.X, ALU.add).then_inc(sq_summed, 1)
                    dve.wait_ge(sq_summed, g + 1)
                    nc.vector.tensor_scalar(ssq[:, :, :], ssq[:, :, :], EPS, None, ALU.add).then_inc(ssq_ready, 1)
                if prepare and j == END + 6:
                    dve.wait_ge(rn_ready, g + 1)
                    for t in range(TILES):
                        nc.vector.tensor_scalar(tok[o][:, t, 0, :], tok[o][:, t, 0, :], rn[:, t, 0:1], P ** -0.5,
                                                ALU.mult, ALU.mult)
                        ins = nc.vector.tensor_scalar(tok[o][:, t, 1, :], tok[o][:, t, 1, :], rn[:, t, 1:2], None, ALU.mult)
                    ins.then_inc(normed, 1)

            def inverses(h, b, scan, prepare):
                dve.wait_ge(vh_ready, h + 1)
                for r, lanes in enumerate(LANES):
                    for l, n in enumerate(lanes):
                        dve.wait_ge(gram, h * NBAT + (n + 1))
                        for a in range(BT):
                            for d in range(2):
                                t = BT * n + a
                                for c in range(2):
                                    vec = GC if c == d else R2
                                    half = slice(c * CH, (c + 1) * CH)
                                    ins = nc.vector.scalar_tensor_tensor(
                                        dm[l][:, a, d, half], flips[l][:, 2 * a + d, half], vh[b][:, vec, d, t:t + 1],
                                        causal[:, d, half], ALU.subtract, ALU.min)
                        ins.then_inc(dm_ready, 1)
                        nc.vector.tensor_copy(sys4(yy[b], n), eye4[:, :, :])
                        nc.vector.tensor_copy(flat(xx[l]), eye4[:, :, :]).then_inc(eye_ready, 1)
                    beside(h, b, r * SLOTS, scan, prepare)
                    for l, n in enumerate(lanes):
                        dve.wait_ge(dec_ready, h * NBAT + (n + 1))
                        for a in range(BT):
                            t = BT * n + a
                            for d in range(2):
                                nc.vector.scalar_tensor_tensor(at[l][:, a, d, :], halves[l][:, 2 * a, :],
                                                               vh[b][:, NBETA, d, t:t + 1], dec[l][:, a, d, :],
                                                               ALU.mult, ALU.mult)
                        for d in range(2):
                            kqt = halves[l][:, :, :].rearrange("p (a s) n -> p a s n", s=2)[:, :, 1, :]
                            ins = nc.vector.tensor_tensor(qk[b][:, BT * n:BT * n + BT, d, :], kqt, dec[l][:, :, d, :], ALU.mult)
                        ins.then_inc(at_ready, 1)
                    for l, n in enumerate(lanes):
                        dve.wait_ge(eye_ready, h * NBAT + (n + 1))
                        dve.wait_ge(at_ready, h * NBAT + (n + 1))
                        dve.wait_ge(at_turned, h * NBAT + (n + 1))
                        dve.sem_inc(passed, 1)
                        for a in range(BT):
                            nc.vector.copy_predicated(yy[b][:, BT * n + a, :, :], upper[:, 0, :, :], at[l][:, a, :, :])
                            ins = nc.vector.copy_predicated(xx[l][:, a, :, :], lower[:, 0, :, :], flips[l][:, 2 * a:2 * a + 2, :])
                        ins.then_inc(xy_ready, 1)
                    beside(h, b, r * SLOTS + 1, scan, prepare)
                    for s in range(1, NL + 1):
                        beside(h, b, r * SLOTS + 2 * s, scan, prepare)
                        for l, n in enumerate(lanes):
                            dve.wait_ge(xy_done, h * (NBAT * NL) + (1 + level_at(lanes, s - 1, l, NL)))
                            dve.sem_inc(passed, 1)
                            for a in range(BT):
                                if s < NL:
                                    nc.vector.copy_predicated(xx[l][:, a, :, :], lower[:, s, :, :], flips[l][:, 2 * a:2 * a + 2, :])
                                ins = nc.vector.copy_predicated(yy[b][:, BT * n + a, :, :], upper[:, s, :, :],
                                                                yprod[l][:, 2 * a:2 * a + 2, :])
                            ins.then_inc(xy_ready, 1)
                        beside(h, b, r * SLOTS + 2 * s + 1, scan, prepare)
            heads(dve, inverses, beside)


def level_at(lanes, s, l, levels):
    return lanes[0] * levels + s * len(lanes) + l


def xy_value(h, n, s, levels):
    lanes = (n - n % 2, n - n % 2 + 1) if n - n % 2 + 1 < TILES // BT else (n,)
    return h * (TILES // BT * (levels + 1)) + (lanes[0] * (levels + 1) + s * len(lanes) + (n - lanes[0]) + 1)


def project_out(nc, sems, layer, A, w_dram, y_dram, res, result, first_tile, final):
    KY = 2 * D // P
    total = TILES - first_tile
    with ExitStack() as ph:
        sb = lambda n, s, d=F32: ph.enter_context(nc.sbuf_tensor(f"{n}_o{layer}", s, d))
        x = [sb(f"x{b}", [P, D]) for b in range(2)]
        w_hi, w_lo = sb("w_hi", [P, KY, D], F32R), sb("w_lo", [P, KY, D], F32R)
        y = sb("y", [P, KY, P])
        y_hi = [sb(f"y_hi{b}", [P, KY, P], F32R) for b in range(2)]
        y_lo = [sb(f"y_lo{b}", [P, KY, P], F32R) for b in range(2)]
        g = sb("g", [P, 1 if final else 2, D])
        t = sb("t", [P, D])
        norm_w = sb("norm_w", [P, D]) if final else None
        mhalf = sb("mhalf", [P, 1])
        ssq, rstd = sb("ssq", [P, 1]), sb("rstd", [P, 1])
        acc = [ph.enter_context(nc.psum_tensor(f"acc{b}_o{layer}", [P, D], F32)) for b in range(2)]
        sem = lambda n: sems(f"{n}_o{layer}")
        w_in = [sem(f"w_in{b}") for b in range(2)]
        x_in = [sem(f"x_in{b}") for b in range(2)]
        g_in, y_in, out_dma = sem("g_in"), sem("y_in"), sem("out_dma")
        w_hi_ready, w_lo_ready, y_hi_ready, y_lo_ready = map(sem, ("w_hi_ready", "w_lo_ready", "y_hi_ready", "y_lo_ready"))
        product, gated, added, half_ready = map(sem, ("product", "gated", "added", "half_ready"))
        ssq_ready, ms_ready, rstd_ready, done = map(sem, ("ssq_ready", "ms_ready", "rstd_ready", "done"))
        block = ph.enter_context(nc.Block())

        def pairs(eng, pair):
            if first_tile == 0:
                pair(0, True, 1)
                with eng.Fori(1, total // 2) as i:
                    pair(i * 2, False, 0)
            else:
                pair(0, True, 0)
                with eng.Fori(1, total // 2) as i:
                    pair(i * 2, False, 0)
        one = lambda rows, i: rows.rearrange("(t p) d -> t p d", p=P)[bass.ds(i, 1), :, :].rearrange("a p d -> (a p) d")
        yv = y_dram.rearrange("(k p) t -> p k t", p=P)
        wv = w_dram.rearrange("(k p) n -> k p n", p=P)

        @block.sync
        def _(sp):
            sp.dma_start(y[:, :, :], yv[:, :, 0:P]).then_inc(y_in, 16)
            for k in range(2):
                sp.dma_start(x[k][:, :], wv[k]).then_inc(w_in[k], 16)
            sp.wait_ge(y_lo_ready, 1)
            sp.dma_start(y[:, :, :], yv[:, :, P:2 * P]).then_inc(y_in, 16)
            for s in range(1 if final else 2):
                sp.dma_start(g[:, s, :], A["mods_dram"][layer, s, :].partition_broadcast(P)).then_inc(g_in, 16)
            if final:
                sp.dma_start(norm_w[:, :], A["final_norm_w"].partition_broadcast(P)).then_inc(g_in, 16)
            for k in range(2, KY):
                sp.wait_ge(w_lo_ready, k - 1)
                sp.dma_start(x[k % 2][:, :], wv[k]).then_inc(w_in[k % 2], 16)
            sp.wait_ge(w_lo_ready, KY)

            def store(n, b):
                sp.wait_ge(done, n + 1)
                sp.dma_start(one(result, n), x[b][:, :]).then_inc(out_dma, 16)

            def pair(n0, first, stream):
                for b in range(2):
                    n = n0 + b
                    if not first:
                        sp.wait_ge(y_lo_ready, n)
                        sp.dma_start(y[:, :, :], yv[:, :, bass.ds(n * P, P)]).then_inc(y_in, 16)
                    if not (first and b == 0):
                        store(n - 1, 1 - b)
                    if not first:
                        sp.wait_ge(out_dma, (n - 1) * 16)
                    sp.dma_start(x[b][:, :], one(res, n + first_tile)).then_inc(x_in[b], 16)
            pairs(sp, pair)
            store(total - 1, 1)
            sp.wait_ge(out_dma, total * 16)

        @block.gpsimd
        def _(pool):
            nc.gpsimd.memset(mhalf[:, :], -0.5).then_inc(half_ready, 1)
            pool.wait_ge(half_ready, 1)
            if final:
                with pool.Fori(0, total) as n:
                    pool.wait_ge(ms_ready, n + 1)
                    nc.gpsimd.tensor_tensor(rstd[:, :], ssq[:, :], mhalf[:, :], ALU.pow).then_inc(rstd_ready, 1)

        @block.tensor
        def _(pe):
            def chunk(b, k):
                for lhs, rhs in ((y_hi[b], w_hi), (y_hi[b], w_lo), (y_lo[b], w_hi)):
                    for a in range(0, D, 512):
                        mm = nc.tensor.matmul(acc[b][:, a:a + 512], lhs[:, k, :], rhs[:, k, a:a + 512],
                                              start=(k == 0 and lhs is y_hi[b] and rhs is w_hi),
                                              stop=(k == KY - 1 and lhs is y_lo[b]))
                return mm

            def pair(n0, first, stream):
                if first:
                    pe.wait_ge(y_lo_ready, 2)
                    for k in range(KY):
                        pe.wait_ge(w_lo_ready, k + 1)
                        for b in range(2):
                            mm = chunk(b, k)
                            if k == KY - 1:
                                mm.then_inc(product, 1)
                    return
                for b in range(2):
                    pe.wait_ge(y_lo_ready, n0 + (b + 1))
                    pe.wait_ge(gated, n0 + (b - 1))
                    for k in range(KY):
                        mm = chunk(b, k)
                    mm.then_inc(product, 1)
            pairs(pe, pair)

        @block.scalar
        def _(act):
            def high(n, b):
                act.wait_ge(y_in, n * 16 + 16)
                nc.scalar.activation(y_hi[b][:, :, :], y[:, :, :], ACT.Copy).then_inc(y_hi_ready, 1)
            high(0, 0)
            high(1, 1)
            for k in range(KY):
                act.wait_ge(w_in[k % 2], 16 * (k // 2 + 1))
                nc.scalar.activation(w_hi[:, k, :], x[k % 2][:, :], ACT.Copy).then_inc(w_hi_ready, 1)

            def square(n, b):
                act.wait_ge(added, n + 1)
                nc.scalar.activation(t[:, :], x[b][:, :], ACT.Square, accum_out=ssq[:, :]).then_inc(ssq_ready, 1)

            def pair(n0, first, stream):
                for b in range(2):
                    if not first:
                        act.wait_ge(product, n0 + (b - 1))
                        high(n0 + b, b)
                    if final and not (first and b == 0):
                        square(n0 + (b - 1), 1 - b)
            pairs(act, pair)
            if final:
                square(total - 1, 1)

        @block.vector
        def _(dve):
            def low(n, b):
                dve.wait_ge(y_hi_ready, n + 1)
                nc.vector.tensor_tensor(y_lo[b][:, :, :], y[:, :, :], y_hi[b][:, :, :].bitcast(F32), ALU.subtract)\
                    .then_inc(y_lo_ready, 1)
            low(0, 0)
            low(1, 1)
            for k in range(KY):
                dve.wait_ge(w_hi_ready, k + 1)
                nc.vector.tensor_tensor(w_lo[:, k, :], x[k % 2][:, :], w_hi[:, k, :].bitcast(F32), ALU.subtract)\
                    .then_inc(w_lo_ready, 1)

            def finish(n, b, half, stream):
                dve.wait_ge(product, n + 1)
                dve.wait_ge(x_in[b], half * 8 + 16)
                if final:
                    dve.wait_ge(half_ready, 1)
                nc.vector.tensor_tensor(t[:, :], acc[b][:, :], g[:, stream, :], ALU.mult).then_inc(gated, 1)
                dve.wait_ge(gated, n + 1)
                ins = nc.vector.tensor_tensor(x[b][:, :], x[b][:, :], t[:, :], ALU.add)
                if not final:
                    ins.then_inc(done, 1)
                    return
                ins.then_inc(added, 1)
                dve.wait_ge(ssq_ready, n + 1)
                nc.vector.tensor_scalar(ssq[:, :], ssq[:, :], 1.0 / D, EPS, ALU.mult, ALU.add).then_inc(ms_ready, 1)
                dve.wait_ge(rstd_ready, n + 1)
                nc.vector.scalar_tensor_tensor(x[b][:, :], x[b][:, :], rstd[:, 0:1], norm_w[:, :], ALU.mult, ALU.mult)\
                    .then_inc(done, 1)

            def pair(n0, first, stream):
                if not first:
                    low(n0 + 1, 1)
                finish(n0, 0, n0, stream)
                nxt(n0)
                finish(n0 + 1, 1, n0, stream)

            def nxt(n0):
                if isinstance(n0, int) and n0 + 2 >= total:
                    return
                low(n0 + 2, 0)
            dve.wait_ge(g_in, 16 * 2)
            if first_tile == 0:
                pair(0, True, 1)
            else:
                pair(0, True, 0)
            with dve.Fori(1, total // 2 - 1) as i:
                pair(i * 2, False, 0)
            pair(total - 2, False, 0)


H_C = 16
DC = 64
LAM_INIT = 0.8 - 0.6 * math.exp(-0.3)


def project_odd(nc, sems, A, h_hi, h_lo):
    N = 16
    NB = 4 * N
    with ExitStack() as ph:
        sb = lambda n, s, d=F32: ph.enter_context(nc.sbuf_tensor(f"{n}_p", s, d))
        cos, sin = sb("cos", [P, T_LAT]), sb("sin", [P, T_LAT])
        w = [sb(f"w{b}", [P, KC, P]) for b in range(2)]
        w_hi = [sb(f"w_hi{b}", [P, KC, P], F32R) for b in range(2)]
        w_lo = [sb(f"w_lo{b}", [P, KC, P], F32R) for b in range(2)]
        raw = [sb(f"raw{b}", [P, T]) for b in range(2)]
        rot = [sb(f"rot{b}", [P, T_LAT]) for b in range(2)]
        hi = [sb(f"hi{b}", [P, T], F32R) for b in range(2)]
        lo = [sb(f"lo{b}", [P, T], F32R) for b in range(2)]
        acc = [ph.enter_context(nc.psum_tensor(f"acc{b}_p", [P, 1536], F32)) for b in range(2)]
        sem = lambda n: sems(f"{n}_p")
        const_in = sem("const_in")
        w_in = [sem(f"w_in{b}") for b in range(2)]
        out_dma = [sem(f"out_dma{b}") for b in range(2)]
        part_dma = [sem(f"part_dma{b}") for b in range(2)]
        w_hi_ready, w_lo_ready, product, acc_read = map(sem, ("w_hi_ready", "w_lo_ready", "product", "acc_read"))
        rot_ready, turned, hi_ready, lo_ready, pstep = map(sem, ("rot_ready", "turned", "hi_ready", "lo_ready", "pstep"))
        block = ph.enter_context(nc.Block())
        w_dram = A["odd_w_in"]
        v_dram = A["v_dram"].rearrange("(n p) t -> n p t", p=P)
        z_dram = A["z1_dram"].rearrange("(n p) t -> n p t", p=P)
        hi_dram = A["kq_hi_dram"].rearrange("(n p) t -> n p t", p=P)
        lo_dram = A["kq_lo_dram"].rearrange("(n p) t -> n p t", p=P)
        one = lambda ap, n: ap[bass.ds(n, 1), :, :].rearrange("a p t -> (a p) t")

        @block.sync
        def _(sp):
            sp.dma_start(cos[:, :], A["rope_cos"]).then_inc(const_in, 16)
            sp.dma_start(sin[:, :], A["rope_sin"]).then_inc(const_in, 16)

            def pair(i, first=False):
                for b in range(2):
                    if not first:
                        sp.wait_ge(w_lo_ready, i * 2 + (b - 1))
                    sp.dma_start(w[b][:, :, :], w_dram[bass.ds(i * 2 + b, 1), :, :, :].rearrange("a p k n -> (a p) k n"))\
                        .then_inc(w_in[b], 16)

            def store_v(i):
                for b in range(2):
                    sp.wait_ge(acc_read, i * 2 + (b + 1))
                    sp.dma_start(one(v_dram, i * 2 + b), raw[b][:, :]).then_inc(out_dma[b], 16)

            def store_parts(i, t0):
                for b in range(2):
                    n = i * 2 + (b - N)
                    sp.wait_ge(lo_ready, n + 1)
                    sp.dma_start(one(hi_dram, n)[:, t0:T], hi[b][:, t0:T].bitcast(F32)).then_inc(part_dma[b], 16)
                    sp.dma_start(one(lo_dram, n)[:, t0:T], lo[b][:, t0:T].bitcast(F32)).then_inc(part_dma[b], 16)

            def store_z(i):
                for b in range(2):
                    sp.wait_ge(acc_read, i * 2 + (b + 1))
                    sp.dma_start(one(z_dram, i * 2 + (b - 3 * N)), raw[b][:, T_CTX:T]).then_inc(out_dma[b], 16)
            H = N // 2
            pair(0, True)
            pair(1)
            with sp.Fori(2, H + 2) as i:
                pair(i)
                store_v(i - 2)
            with sp.Fori(H + 2, 2 * H + 2) as i:
                pair(i)
                store_parts(i - 2, 0)
            with sp.Fori(2 * H + 2, 3 * H + 2) as i:
                pair(i)
                store_parts(i - 2, T_CTX)
            with sp.Fori(3 * H + 2, 4 * H) as i:
                pair(i)
                store_z(i - 2)
            store_z(4 * H - 2)
            store_z(4 * H - 1)
            for b in range(2):
                sp.wait_ge(out_dma[b], 16 * N)
                sp.wait_ge(part_dma[b], 32 * N)

        @block.tensor
        def _(pe):
            def multiply(n, b, first, t0):
                pe.wait_ge(w_lo_ready, n + 1)
                if not first:
                    pe.wait_ge(acc_read, n - 1)
                products(nc, acc[b], w_hi[b], w_lo[b], h_hi, h_lo, t0, T).then_inc(product, 1)
            for b in range(2):
                multiply(b, b, True, 0)
            with pe.Fori(1, N) as i:
                for b in range(2):
                    multiply(i * 2 + b, b, False, 0)
            with pe.Fori(N, 2 * N) as i:
                for b in range(2):
                    multiply(i * 2 + b, b, False, T_CTX)

        @block.scalar
        def _(act):
            def high(n, b, first=False):
                act.wait_ge(w_in[b], (n - b) * 8 + 16)
                if not first:
                    act.wait_ge(product, n - 1)
                nc.scalar.activation(w_hi[b][:, :, :], w[b][:, :, :], ACT.Copy).then_inc(w_hi_ready, 1)

            def evacuate(n, b, fn, t0, scale=1.0):
                act.wait_ge(product, n + 1)
                nc.scalar.activation(raw[b][:, t0:T], acc[b][:, 0:T - t0], fn, scale=scale).then_inc(acc_read, 1)

            def part(m, b, t0, fresh=False):
                act.wait_ge(turned, m + 1)
                if not fresh:
                    act.wait_ge(part_dma[b], (m - b) * 16)
                nc.scalar.activation(hi[b][:, t0:T], raw[b][:, t0:T], ACT.Copy).then_inc(hi_ready, 1)

            high(0, 0, True)
            for b in range(2):
                high(b + 1, 1 - b, b == 0)
                evacuate(b, b, ACT.Copy, 0)
            with act.Fori(1, N // 2) as i:
                for b in range(2):
                    high(i * 2 + (b + 1), 1 - b)
                    act.wait_ge(out_dma[b], i * 16)
                    evacuate(i * 2 + b, b, ACT.Copy, 0)

            def rotated(i, fresh, t0, scale, prev_t0):
                for b in range(2):
                    n = i * 2 + b
                    high(n + 1, 1 - b)
                    if fresh:
                        act.wait_ge(out_dma[b], 8 * N)
                    else:
                        act.wait_ge(lo_ready, n - (N + 1))
                    act.wait_ge(rot_ready, n - (N - 1))
                    evacuate(n, b, ACT.Copy, t0, scale)
                    if b:
                        part(n - (N + 1), 0, t0, fresh)
                    elif not fresh:
                        part(n - (N + 1), 1, prev_t0, i == N // 2 + 1 if isinstance(i, int) else False)
            rotated(N // 2, True, 0, 1.0, 0)
            rotated(N // 2 + 1, False, 0, 1.0, 0)
            with act.Fori(N // 2 + 2, N) as i:
                rotated(i, False, 0, 1.0, 0)
            rotated(N, False, T_CTX, DC ** -0.5, 0)
            with act.Fori(N + 1, 3 * N // 2) as i:
                rotated(i, False, T_CTX, DC ** -0.5, T_CTX)

            def silu(i, last, first):
                for b in range(2):
                    n = i * 2 + b
                    if not (last and b):
                        high(n + 1, 1 - b)
                    act.wait_ge(lo_ready, 2 * N - 1 + b) if first else act.wait_ge(out_dma[b], (i - 3 * N // 2) * 16 + 8 * N)
                    evacuate(n, b, ACT.Silu, T_CTX)
                    if first and b == 0:
                        part(2 * N - 1, 1, T_CTX)
            silu(3 * N // 2, False, True)
            with act.Fori(3 * N // 2 + 1, 2 * N - 1) as i:
                silu(i, False, False)
            silu(2 * N - 1, True, False)

        @block.vector
        def _(dve):
            dve.wait_ge(const_in, 32)

            def low(n, b):
                dve.wait_ge(w_hi_ready, n + 1)
                nc.vector.tensor_tensor(w_lo[b][:, :, :], w[b][:, :, :], w_hi[b][:, :, :].bitcast(F32),
                                        ALU.subtract).then_inc(w_lo_ready, 1)

            def rotate(n, b, first, t0, scale):
                dve.wait_ge(product, n + 1)
                if not first:
                    dve.wait_ge(turned, n - (N + 1))
                a = T_CTX - t0
                for g in range(4):
                    src, dst = slice(32 * g, 32 * g + 32), slice(32 * (g ^ 1), 32 * (g ^ 1) + 32)
                    ins = nc.vector.scalar_tensor_tensor(rot[b][dst, :], acc[b][src, a:a + T_LAT], scale, sin[src, :],
                                                         ALU.mult, ALU.mult)
                ins.then_inc(rot_ready, 1)

            low(0, 0)
            with dve.Fori(0, N // 2) as i:
                for b in range(2):
                    low(i * 2 + (b + 1), 1 - b)

            def turn(i, first, t0, scale):
                for b in range(2):
                    low(i * 2 + (b + 1), 1 - b)
                    rotate(i * 2 + b, b, first, t0, scale)
            turn(N // 2, True, 0, 1.0)
            with dve.Fori(N // 2 + 1, N) as i:
                turn(i, False, 0, 1.0)
            with dve.Fori(N, 3 * N // 2) as i:
                turn(i, False, T_CTX, DC ** -0.5)
            with dve.Fori(3 * N // 2, 2 * N - 1) as i:
                for b in range(2):
                    low(i * 2 + (b + 1), 1 - b)
            low(NB - 1, 1)

        @block.gpsimd
        def _(pool):
            pool.wait_ge(const_in, 32)
            step = Count(pstep)

            def turn(m, b, t0):
                lat = raw[b][:, T_CTX:T]
                pool.wait_ge(acc_read, m + (N + 1))
                pool.wait_ge(rot_ready, m + 1)
                link(pool, step, nc.gpsimd.tensor_tensor(lat, lat, cos[:, :], ALU.mult))
                nc.gpsimd.tensor_tensor(lat, lat, rot[b][:, :], ALU.add).then_inc(turned, 1)
                pool.wait_ge(hi_ready, m + 1)
                nc.gpsimd.tensor_tensor(lo[b][:, t0:T], raw[b][:, t0:T], hi[b][:, t0:T].bitcast(F32), ALU.subtract)\
                    .then_inc(lo_ready, 1)
            for i0, i1, t0 in ((0, N // 2, 0), (N // 2, N, T_CTX)):
                with pool.Fori(i0, i1) as i:
                    step.loop(i - i0, 2)
                    for b in range(2):
                        turn(i * 2 + b, b, t0)
                step.end(i1 - i0)


QT = LAT_TILES
SUBLN_SCALE = 1.0 - LAM_INIT
GROUPS = ((0, 4), (4, 8), (8, TILES))


def attention(nc, sems, A):
    with ExitStack() as ph:
        sb = lambda n, s, d=F32: ph.enter_context(nc.sbuf_tensor(f"{n}_t", s, d))
        ident = sb("ident", [P, P])
        lam_v, lam_p, lam_s, neg_lam = sb("lam_v", [P, 4, DC]), sb("lam_p", [P, 2, DC]), sb("lam_s", [P, 2]), sb("neg_lam", [P, 1])
        norm_w, mhalf = sb("norm_w", [P, 1]), sb("mhalf", [P, QT])
        q = [[sb(f"q{b}{m}", [P, T_LAT], F32R) for m in range(2)] for b in range(2)]
        k_hi = [[sb(f"k_hi{b}{m}", [P, T], F32R) for m in range(2)] for b in range(2)]
        k_lo = [[sb(f"k_lo{b}{m}", [P, T], F32R) for m in range(2)] for b in range(2)]
        v_turn = sb("v_turn", [P, T])
        gate = sb("gate", [P, T_LAT])
        v = [sb(f"v{b}", [P, TILES, 2, P], F32R) for b in range(2)]
        prob = [[sb(f"prob{b}{m}", [P, T]) for m in range(2)] for b in range(2)]
        a_hi = [sb(f"a_hi{b}", [P, TILES, P], F32R) for b in range(2)]
        a_lo = [sb(f"a_lo{b}", [P, TILES, P], F32R) for b in range(2)]
        nmax, total = (sb(n, [P, 2, 2]) for n in ("nmax", "total"))
        rec, ratio = sb("rec", [P, 4, 2]), sb("ratio", [P, 2])
        o = [sb(f"o{b}", [P, QT, 2, P]) for b in range(2)]
        ossq, orn = sb("ossq", [P, QT]), sb("orn", [P, QT])
        yt = sb("yt", [P, T_LAT])
        sc = [ph.enter_context(nc.psum_tensor(f"scores{m}_t", [P, 1536], F32)) for m in range(2)]
        ring = [ph.enter_context(nc.psum_tensor(f"ring{m}_t", [P, 4, P], F32)) for m in range(2)]
        sem = lambda n: sems(f"{n}_t")
        const_in, lam_step, lam_exp, lam_ready, half_ready = map(sem, ("const_in", "lam_step", "lam_exp", "lam_ready", "half_ready"))
        qk_in = [sem(f"qk_in{b}") for b in range(2)]
        v_in, gate_in, y_out = map(sem, ("v_in", "gate_in", "y_out"))
        scored = [sem(f"scored{m}") for m in range(2)]
        max_ready = [sem(f"max_ready{m}") for m in range(2)]
        exped = [sem(f"exped{m}") for m in range(2)]
        v_turned, v_hi_ready, v_lo_ready, a_turned, a_hi_ready, a_lo_ready = map(
            sem, ("v_turned", "v_hi_ready", "v_lo_ready", "a_turned", "a_hi_ready", "a_lo_ready"))
        rec_ready, ratio_ready, diff_ready, valued, o_ready = map(
            sem, ("rec_ready", "ratio_ready", "diff_ready", "valued", "o_ready"))
        o_sum, osq_ready, ossq_sum, ossq_ready, orn_ready, oscaled, o_turned, y_ready = map(
            sem, ("o_sum", "osq_ready", "ossq_sum", "ossq_ready", "orn_ready", "oscaled", "o_turned", "y_ready"))
        block = ph.enter_context(nc.Block())
        U = 2 * QT

        def steps(eng, step, drain):
            for u in range(U):
                step(0, u, u)
            with eng.Fori(1, H_C // 2) as i:
                for u in range(U):
                    step(i, u, U)
            drain()
        unit = lambda i, u: i * U + u
        head = lambda i, u: i * 2 + u // QT

        @block.sync
        def _(sp):
            sp.dma_start(ident[:, :], A["identity"]).then_inc(const_in, 16)
            sp.dma_start(norm_w[:, :], A["odd_subln_w"]).then_inc(const_in, 16)
            sp.dma_start(lam_v[:, :, :], A["odd_lambda"].partition_broadcast(P)).then_inc(const_in, 16)
            hi = A["kq_hi_dram"].rearrange("(s h m c) t -> s h m c t", s=2, m=2, c=DC)
            lo = A["kq_lo_dram"].rearrange("(s h m c) t -> s h m c t", s=2, m=2, c=DC)
            vd = A["v_dram"].rearrange("(h p) t -> h p t", p=P)
            zd = A["z1_dram"].rearrange("(h p) t -> h p t", p=P)
            yd = A["y1_dram"].rearrange("(h p) t -> h p t", p=P)
            one = lambda ap, h: ap[bass.ds(h, 1), :, :].rearrange("a p t -> (a p) t")

            def load(h, b):
                for m in range(2):
                    for dst, srcs, t0 in ((q[b][m], (hi[1], lo[1]), T_CTX), (k_hi[b][m], (hi[0], hi[0]), 0),
                                          (k_lo[b][m], (lo[0], lo[0]), 0)):
                        for j, src in enumerate(srcs):
                            sp.dma_start(dst[j * DC:(j + 1) * DC, :].bitcast(F32), src[bass.ds(h, 1), m, :, t0:T]
                                         .rearrange("a c t -> (a c) t")).then_inc(qk_in[b], 16)

            def load_v(h):
                sp.dma_start(v_turn[:, :], one(vd, h)).then_inc(v_in, 16)

            def load_gate(h):
                sp.dma_start(gate[:, :], one(zd, h)).then_inc(gate_in, 16)

            def store(h):
                sp.wait_ge(y_ready, h * 2 + 2)
                sp.dma_start(one(yd, h), yt[:, :]).then_inc(y_out, 16)
            load(0, 0)
            load_v(0)
            load_gate(0)
            load(1, 1)
            sp.wait_ge(v_turned, 3)
            load_v(1)
            with sp.Fori(1, H_C // 2) as i:
                for b in range(2):
                    h = i * 2 + b
                    sp.wait_ge(scored[1], h * QT - QT)
                    load(h, b)
                    sp.wait_ge(v_turned, h * 3)
                    load_v(h)
                    store(h - 2)
                    load_gate(h - 1)
            store(H_C - 2)
            load_gate(H_C - 1)
            store(H_C - 1)
            sp.wait_ge(y_out, 16 * H_C)

        @block.tensor
        def _(pe):
            pe.wait_ge(const_in, 48)
            reader = [None, None]

            def take(r, i, sem, per, value):
                if reader[r]:
                    last, grows, at = reader[r]
                    pe.wait_ge(last, i * grows + at)
                reader[r] = (sem, per, value)
                return ring[r]

            def turn_values(i, u):
                pe.wait_ge(v_in, head(i, u) * 16 + 16)
                for n, (a, b) in enumerate(GROUPS):
                    bank = take(n % 2, i, v_lo_ready, 6, u // QT * 3 + n + 1)
                    for t in range(a, b):
                        mm = nc.tensor.transpose(bank[:, t - a, :], v_turn[:, t * P:(t + 1) * P], ident[:, :])
                    mm.then_inc(v_turned, 1)

            def score(i, u, lag):
                g, b, t = unit(i, u), u // QT, u % QT
                if t == 0:
                    pe.wait_ge(qk_in[b], i * 192 + 192)
                for m in range(2):
                    if lag:
                        pe.wait_ge(exped[m], g)
                    for k in (k_hi[b][m], k_lo[b][m]):
                        for a in range(0, T, 512):
                            e = min(a + 512, T)
                            mm = nc.tensor.matmul(sc[m][:, a:e], q[b][m][:, t * P:(t + 1) * P], k[:, a:e],
                                                  start=(k is k_hi[b][m]), stop=(k is k_lo[b][m]))
                    mm.then_inc(scored[m], 1)

            def turn_difference(i, u):
                par = u % 2
                pe.wait_ge(diff_ready, unit(i, u) + 1)
                for n, (a, b) in enumerate(GROUPS):
                    bank = take(n % 2, i, a_lo_ready, 3 * U, 3 * u + n + 1)
                    for t in range(a, b):
                        mm = nc.tensor.transpose(bank[:, t - a, :], prob[par][0][:, t * P:(t + 1) * P], ident[:, :])
                    mm.then_inc(a_turned, 1)

            def value(i, u):
                par, b = u % 2, u % U // QT
                pe.wait_ge(a_lo_ready, unit(i, u) * 3 + 3)
                bank = take(1, i, o_ready, U, u + 1)
                for t in range(TILES):
                    for a in (a_hi[par], a_lo[par]):
                        mm = nc.tensor.matmul(bank[:, 0:2, :], a[:, t, :], v[b][:, t, :, :],
                                              start=(t == 0 and a is a_hi[par]), stop=(t == TILES - 1 and a is a_lo[par]))
                mm.then_inc(valued, 1)

            def turn_output(i, j):
                b = j % 2
                pe.wait_ge(oscaled, i * 2 + (j + 1))
                for n in range(2):
                    bank = take(n, i, y_ready, 4, 2 * j + n + 1)
                    for t in range(4):
                        mm = nc.tensor.transpose(bank[:, t, :], o[b][:, 4 * n + t, 0, :], ident[:, :])
                    mm.then_inc(o_turned, 1)

            def step(i, u, lag):
                if u % QT == 0:
                    turn_values(i, u)
                score(i, u, lag)
                if u % QT == 0:
                    pe.wait_ge(v_lo_ready, head(i, u) * 3 + 3)
                if lag >= 1:
                    turn_difference(i, u - 1)
                if lag >= 2:
                    value(i, u - 2)
                if u % QT == 5 and lag >= QT:
                    turn_output(i, u // QT - 1)
                if u == U - 1:
                    for r in range(2):
                        last, grows, at = reader[r]
                        reader[r] = (last, grows, at - grows)

            def drain():
                i = H_C // 2
                turn_difference(i, -1)
                value(i, -2)
                value(i, -1)
                turn_output(i, -1)
            steps(pe, step, drain)

        @block.scalar
        def _(act):
            act.wait_ge(lam_step, 2)
            nc.scalar.activation(lam_s[:, :], lam_s[:, :], ACT.Exp).then_inc(lam_exp, 1)

            def values_high(i, u, lag):
                h = head(i, u)
                for n, (a, b) in enumerate(GROUPS):
                    act.wait_ge(v_turned, h * 3 + (n + 1))
                    if lag >= U:
                        act.wait_ge(valued, h * QT - QT)
                    nc.scalar.activation(v[u // QT][:, a:b, 0, :], ring[n % 2][:, 0:b - a, :], ACT.Copy).then_inc(v_hi_ready, 1)

            def exponent(i, u, lag, m):
                g, par = unit(i, u), u % 2
                act.wait_ge(max_ready[m], g + 1)
                if lag >= 2:
                    act.wait_ge(a_turned, g * 3 - 3)
                    act.wait_ge(ratio_ready, g - 1)
                nc.scalar.activation(prob[par][m][:, :], sc[m][:, 0:T], ACT.Exp, bias=nmax[:, par, m:m + 1],
                                     accum_out=total[:, par, m:m + 1]).then_inc(exped[m], 1)

            def difference_high(g, par, fresh, groups):
                for n in groups:
                    a, b = GROUPS[n]
                    act.wait_ge(a_turned, g * 3 + (n + 1))
                    if not fresh:
                        act.wait_ge(valued, g - 1)
                    nc.scalar.activation(a_hi[par][:, a:b, :], ring[n % 2][:, 0:b - a, :], ACT.Copy).then_inc(a_hi_ready, 1)

            def output(g, b, t, turned=None):
                act.wait_ge(valued, g + 1)
                if turned is not None:
                    act.wait_ge(o_turned, turned)
                nc.scalar.activation(o[b][:, t, :, :], ring[1][:, 0:2, :], ACT.Copy, scale=rec[:, t % 4, 0:1]).then_inc(o_ready, 1)

            def square(h, b):
                act.wait_ge(o_sum, h + 1)
                nc.scalar.activation(o[b][:, :, 1, :], o[b][:, :, 0, :], ACT.Square).then_inc(osq_ready, 1)

            def step(i, u, lag):
                if u % QT == 0:
                    values_high(i, u, lag)
                last = unit(i, u - 1), (u - 1) % 2, lag < 3
                if lag >= 1:
                    difference_high(*last, (0, 1))
                exponent(i, u, lag, 0)
                if lag >= 1:
                    difference_high(*last, (2,))
                exponent(i, u, lag, 1)
                if lag >= 2:
                    t = (u - 2) % U
                    output(unit(i, u - 2), t // QT, t % QT, head(i, u) * 2 - 2 if t % QT == 0 and lag >= U else None)
                if u % QT == 3 and lag >= QT:
                    square(head(i, u) - 1, 1 - u // QT)

            def drain():
                n = H_C * QT
                difference_high(n - 1, 1, False, (0, 1, 2))
                output(n - 2, 1, QT - 2)
                output(n - 1, 1, QT - 1)
                square(H_C - 1, 1)
            steps(act, step, drain)

        @block.vector
        def _(dve):
            dve.wait_ge(const_in, 48)
            nc.vector.tensor_scalar(norm_w[:, :], norm_w[:, :], SUBLN_SCALE, None, ALU.mult)
            nc.vector.tensor_tensor(lam_p[:, :, :], lam_v[:, 0::2, :], lam_v[:, 1::2, :], ALU.mult).then_inc(lam_step, 1)
            dve.wait_ge(lam_step, 1)
            nc.vector.tensor_reduce(lam_s[:, :], lam_p[:, :, :], AX.X, ALU.add).then_inc(lam_step, 1)
            dve.wait_ge(lam_exp, 1)
            nc.vector.tensor_tensor(neg_lam[:, :], lam_s[:, 1:2], lam_s[:, 0:1], ALU.subtract).then_inc(lam_ready, 1)
            dve.wait_ge(lam_ready, 1)
            nc.vector.tensor_scalar(neg_lam[:, :], neg_lam[:, :], LAM_INIT, None, ALU.subtract).then_inc(lam_ready, 1)
            dve.wait_ge(lam_ready, 2)

            def values_low(i, u):
                h = head(i, u)
                for n, (a, b) in enumerate(GROUPS):
                    dve.wait_ge(v_hi_ready, h * 3 + (n + 1))
                    nc.vector.tensor_tensor(v[u // QT][:, a:b, 1, :], ring[n % 2][:, 0:b - a, :],
                                            v[u // QT][:, a:b, 0, :].bitcast(F32), ALU.subtract)\
                        .then_inc(v_lo_ready, 1)

            def maximum(i, u, m):
                dve.wait_ge(scored[m], unit(i, u) + 1)
                nc.vector.tensor_reduce(nmax[:, u % 2, m:m + 1], sc[m][:, 0:T], AX.X, ALU.max, negate=True)\
                    .then_inc(max_ready[m], 1)

            def difference_low(g, par, groups):
                for n in groups:
                    a, b = GROUPS[n]
                    dve.wait_ge(a_hi_ready, g * 3 + (n + 1))
                    nc.vector.tensor_tensor(a_lo[par][:, a:b, :], ring[n % 2][:, 0:b - a, :],
                                            a_hi[par][:, a:b, :].bitcast(F32), ALU.subtract)\
                        .then_inc(a_lo_ready, 1)

            def mix(i, u, lag):
                g, par = unit(i, u), u % 2
                for m in range(2):
                    dve.wait_ge(exped[m], g + 1)
                if lag >= 4:
                    dve.wait_ge(o_ready, g - 3)
                nc.vector.reciprocal(rec[:, u % 4, :], total[:, par, :]).then_inc(rec_ready, 1)
                dve.wait_ge(rec_ready, g + 1)
                nc.vector.scalar_tensor_tensor(ratio[:, par:par + 1], total[:, par, 0:1], rec[:, u % 4, 1:2], neg_lam[:, :],
                                               ALU.mult, ALU.mult).then_inc(ratio_ready, 1)
                dve.wait_ge(ratio_ready, g + 1)
                nc.vector.scalar_tensor_tensor(prob[par][0][:, :], prob[par][1][:, :], ratio[:, par:par + 1],
                                               prob[par][0][:, :], ALU.mult, ALU.add).then_inc(diff_ready, 1)

            def sum_squares(h, b):
                dve.wait_ge(osq_ready, h + 1)
                nc.vector.tensor_reduce(ossq[:, :], o[b][:, :, 1, :], AX.X, ALU.add).then_inc(ossq_sum, 1)
                dve.wait_ge(ossq_sum, h + 1)
                nc.vector.tensor_scalar(ossq[:, :], ossq[:, :], 1.0 / P, EPS, ALU.mult, ALU.add).then_inc(ossq_ready, 1)

            def scale_output(h, b):
                dve.wait_ge(orn_ready, h + 1)
                for t in range(QT):
                    ins = nc.vector.tensor_scalar(o[b][:, t, 0, :], o[b][:, t, 0, :], orn[:, t:t + 1], None, ALU.mult)
                ins.then_inc(oscaled, 1)

            def finish(h, fresh):
                dve.wait_ge(gate_in, h * 16 + 16)
                if not fresh:
                    dve.wait_ge(y_out, h * 16)
                for n in range(2):
                    dve.wait_ge(o_turned, h * 2 + (n + 1))
                    half = slice(4 * n * P, 4 * (n + 1) * P)
                    nc.vector.scalar_tensor_tensor(yt[:, half], ring[n][:, :, :].rearrange("p a n -> p (a n)"),
                                                         norm_w[:, 0:1], gate[:, half], ALU.mult, ALU.mult)\
                        .then_inc(y_ready, 1)

            def step(i, u, lag):
                if u % QT == 0:
                    values_low(i, u)
                if u % QT == 5 and lag >= QT:
                    scale_output(head(i, u) - 1, 1 - u // QT)
                if u % QT == 6 and lag >= QT:
                    finish(head(i, u) - 1, lag < U)
                maximum(i, u, 0)
                if lag >= 1:
                    difference_low(unit(i, u - 1), (u - 1) % 2, (0, 1))
                maximum(i, u, 1)
                if lag >= 1:
                    difference_low(unit(i, u - 1), (u - 1) % 2, (2,))
                mix(i, u, lag)
                if u % QT == 3 and lag >= QT:
                    sum_squares(head(i, u) - 1, 1 - u // QT)

            def drain():
                difference_low(H_C * QT - 1, 1, (0, 1, 2))
                sum_squares(H_C - 1, 1)
                scale_output(H_C - 1, 1)
                finish(H_C - 1, False)
            steps(dve, step, drain)

        @block.gpsimd
        def _(pool):
            nc.gpsimd.memset(mhalf[:, :], -0.5).then_inc(half_ready, 1)
            pool.wait_ge(half_ready, 1)

            def add_parts(h, b):
                pool.wait_ge(o_ready, h * QT + QT)
                nc.gpsimd.tensor_tensor(o[b][:, :, 0, :], o[b][:, :, 0, :], o[b][:, :, 1, :], ALU.add).then_inc(o_sum, 1)

            def root(h):
                pool.wait_ge(ossq_ready, h + 1)
                nc.gpsimd.tensor_tensor(orn[:, :], ossq[:, :], mhalf[:, :], ALU.pow).then_inc(orn_ready, 1)

            add_parts(0, 0)
            root(0)
            add_parts(1, 1)
            root(1)
            with pool.Fori(1, H_C // 2) as i:
                for b in range(2):
                    add_parts(i * 2 + b, b)
                    root(i * 2 + b)


def build(nc, A):
    def stage(function, *args):
        with semaphores(nc) as sems:
            function(nc, sems, *args)

    with ExitStack() as ctx:
        mods = ctx.enter_context(nc.sbuf_tensor("mods", [P, 2, 2 * KC, 2], F32))
        for layer in range(2):
            stage(modulation, layer, A, mods)
        with ExitStack() as l0:
            h_hi = l0.enter_context(nc.sbuf_tensor("h_hi0", [P, KC, T], F32R))
            h_lo = l0.enter_context(nc.sbuf_tensor("h_lo0", [P, KC, T], F32R))
            stage(normalise, 0, A, mods, h_hi, h_lo, A["x"])
            stage(project_even, A, h_hi, h_lo)
        with ExitStack() as l0:
            vt = l0.enter_context(nc.sbuf_tensor("vt", [P, VECS, 2, HT], F32))
            stage(decay_vectors, A, vt)
            stage(deltanet, A, vt)
        stage(project_out, 0, A, A["even_w_out"], A["y_dram"], A["x"], A["stream_dram"], 0, False)
        with ExitStack() as l1:
            h_hi = l1.enter_context(nc.sbuf_tensor("h_hi1", [P, KC, T], F32R))
            h_lo = l1.enter_context(nc.sbuf_tensor("h_lo1", [P, KC, T], F32R))
            stage(normalise, 1, A, mods, h_hi, h_lo, A["stream_dram"])
            stage(project_odd, A, h_hi, h_lo)
        stage(attention, A)
        stage(project_out, 1, A, A["odd_w_out"], A["y1_dram"], A["stream_dram"], A["out"], CTX_TILES, True)


SCRATCH = "Internal"
INS = ["x", "c", "c_ctx", "norm_w", "mod_w", "mod_b", "even_w_in", "even_dn_conv_w", "even_dn_a_log",
       "even_dn_dt_bias", "even_dn_norm_w", "even_sc_conv_w", "even_w_out", "odd_w_in", "odd_lambda",
       "odd_subln_w", "odd_w_out", "final_norm_w", "identity", "decay_consts", "eye4", "causal", "lower", "upper", "rope_cos", "rope_sin"]


def kernel(**inputs):
    import numpy as np
    import concourse.bacc as bacc
    from concourse.bass_utils import run_bass_kernel_spmd as run

    nc = bacc.Bacc("TRN2", target_bir_lowering=False, num_devices=1)
    arrays, A = {}, {}
    columns = lambda v: np.ascontiguousarray(np.swapaxes(v.reshape(*v.shape[:-1], -1, P), -1, 0).reshape(P, -1)) \
        if v.ndim == 1 else np.ascontiguousarray(np.moveaxis(v.reshape(*v.shape[:-1], -1, P), -1, 0))
    inputs = {k: np.asarray(v) for k, v in inputs.items()}
    inputs["c"] = columns(inputs["c"][0])
    inputs["c_ctx"] = columns(inputs["c_ctx"])
    inputs["x"] = np.concatenate([inputs.pop("ctx")[0], inputs["x"][0]])
    inputs["even_w_out"], inputs["odd_w_out"] = inputs["even_w_out"][0], inputs["odd_w_out"][0]
    for name in ("norm_w", "even_dn_conv_w", "even_sc_conv_w"):
        inputs[name] = columns(inputs[name].reshape(-1, inputs[name].shape[-1]))
    w = inputs["even_w_in"][0]
    starts = [128 * n for n in range(32)] + [4128 + g * 1024 + j * 128 for j in range(8) for g in range(4)] + [4096]
    inputs["even_w_in"] = np.stack([w[:, a:a + P].reshape(KC, P, P).transpose(1, 0, 2) for a in starts])
    rows = lambda u: np.repeat(u.reshape(2, H_A).T, TILES, axis=0)
    inputs["decay_consts"] = np.concatenate([rows(inputs["even_dn_dt_bias"]), rows(inputs["even_dn_a_log"])], axis=1)
    inputs["even_dn_norm_w"] = inputs["even_dn_norm_w"].reshape(P, 1)
    inputs["eye4"] = np.ascontiguousarray(np.repeat(np.eye(P, dtype=np.float32)[:, None, :], 4, axis=1))
    r, c = np.arange(P)[:, None], np.arange(P)[None, :]
    inputs["causal"] = np.stack([np.where(c >= r, 0, -1e30), np.where(c <= r, 0, -1e30)], axis=1).astype(np.float32)
    below = np.stack([(r // s == c // s + 1) & (r // s % 2 == 1) for s in LEVELS], axis=1)
    above = np.stack([(c // s == r // s + 1) & (c // s % 2 == 1) for s in LEVELS], axis=1)
    inputs["lower"] = np.stack([below, above], axis=2).astype(np.uint32)
    inputs["upper"] = np.stack([above, below], axis=2).astype(np.uint32)
    order = np.concatenate([np.arange(0, 16), np.arange(32, 48), np.arange(16, 32), np.arange(48, 64)])
    w = inputs["odd_w_in"][0].reshape(D, 4, H_C, 2 * DC)
    maps = w[:, 0:2].reshape(D, 2, H_C, 2, DC)[..., order].reshape(D, 2, H_C, 2 * DC)
    blocks = [w[:, 2], maps[:, 1], maps[:, 0], w[:, 3]]
    inputs["odd_w_in"] = np.concatenate([u.transpose(1, 0, 2).reshape(H_C, KC, P, P).transpose(0, 2, 1, 3) for u in blocks])
    inputs["odd_lambda"] = inputs["odd_lambda"][0]
    inputs["odd_subln_w"] = inputs["odd_subln_w"].reshape(P, 1)
    token = np.arange(T_LAT)
    inv = (np.float32(10000.0) ** (-np.arange(0, DC // 2, 2, dtype=np.float32) / np.float32(DC // 2))).astype(np.float32)
    angle = np.concatenate([(token // 64).astype(np.float32)[:, None] * inv, (token % 64).astype(np.float32)[:, None] * inv], axis=1).T
    inputs["rope_cos"] = np.tile(np.cos(angle), (4, 1)).astype(np.float32)
    sign = np.repeat(np.array([1, -1, 1, -1], dtype=np.float32), DC // 2)[:, None]
    inputs["rope_sin"] = (np.tile(np.sin(angle), (4, 1)) * sign).astype(np.float32)
    inputs["identity"] = np.eye(P, dtype=np.float32)
    for name in INS:
        a = np.ascontiguousarray(inputs[name])
        arrays["in_" + name] = a
        A[name] = nc.dram_tensor("in_" + name, a.shape, mybir.dt.from_np(a.dtype), kind="ExternalInput").ap()
    A["mods_dram"] = nc.dram_tensor("mods_dram", (2, 2, D), F32, kind=SCRATCH).ap()
    for name, rows in (("conv_dram", 3072), ("z_dram", 1024), ("y_dram", 2048), ("ab_dram", 32)):
        A[name] = nc.dram_tensor(name, (rows, T), F32, kind=SCRATCH).ap()
    A["stream_dram"] = nc.dram_tensor("stream_dram", (T, D), F32, kind=SCRATCH).ap()
    for name, rows, cols in (("v_dram", 2048, T), ("z1_dram", 2048, T_LAT), ("y1_dram", 2048, T_LAT),
                             ("kq_hi_dram", 4096, T), ("kq_lo_dram", 4096, T)):
        A[name] = nc.dram_tensor(name, (rows, cols), F32, kind="Internal").ap()
    A["out"] = nc.dram_tensor("out", (T_LAT, D), F32, kind="ExternalOutput").ap()
    build(nc, A)
    r = run(nc, [arrays], core_ids=[0])
    return r.results[0]["out"].reshape(1, T_LAT, D)
```
